# Optimizing a Trainium2 kernel written in Bass

```python
import jax, jax.numpy as jnp
from jax import lax
import numpy as np

D_MODEL = 1024
BATCH = 1
SEQ = 512
DEPTH = 1

CHUNK = 64
N_PREV_CHUNKS = 8
BAND_CHUNKS = N_PREV_CHUNKS + 1
N_HEADS = 16
HEAD_DIM = 64
D_ATTN = N_HEADS * HEAD_DIM
D_CONV = D_MODEL
CONV_WIDTH = 3
MAX_REL = 256
D_FF = 4 * D_MODEL
N_BRANCHES = 2
EPS = 1e-6
NEG_INF = -1e30


def rms_norm(x, g):
    xf = x.astype(jnp.float32)
    y = xf * lax.rsqrt(jnp.mean(xf * xf, axis=-1, keepdims=True) + EPS)
    return (y * g.astype(jnp.float32)).astype(x.dtype)

def chunk_band(t):
    b, nc, c, h, dh = t.shape
    tp = jnp.pad(t, ((0, 0), (N_PREV_CHUNKS, 0), (0, 0), (0, 0), (0, 0)))
    band = jnp.stack([tp[:, o:o + nc] for o in range(BAND_CHUNKS)], axis=2)
    return band.reshape(b, nc, BAND_CHUNKS * c, h, dh)

def chunked_relpos_attention(q, k, v, q_norm_g, k_norm_g, rel_bias):
    b, s, _ = q.shape
    nc = s // CHUNK
    kw = BAND_CHUNKS * CHUNK
    q = rms_norm(q.reshape(b, nc, CHUNK, N_HEADS, HEAD_DIM), q_norm_g)
    k = rms_norm(k.reshape(b, nc, CHUNK, N_HEADS, HEAD_DIM), k_norm_g)
    v = v.reshape(b, nc, CHUNK, N_HEADS, HEAD_DIM)
    kb = chunk_band(k)
    vb = chunk_band(v)

    q_idx = jnp.arange(CHUNK)[:, None]
    k_idx = jnp.arange(kw)[None, :]
    dist = q_idx - k_idx + N_PREV_CHUNKS * CHUNK
    rel_idx = jnp.clip(dist, -MAX_REL, MAX_REL) + MAX_REL
    bias = rel_bias[:, rel_idx].astype(jnp.float32)

    key_chunk = jnp.arange(nc)[:, None] + (jnp.arange(kw) // CHUNK)[None, :] - N_PREV_CHUNKS
    valid = key_chunk >= 0

    scale = HEAD_DIM ** -0.5
    scores = jnp.einsum('bnqhd,bnkhd->bnhqk', q, kb).astype(jnp.float32) * scale
    scores = scores + bias[None, None]
    scores = jnp.where(valid[None, :, None, None, :], scores, NEG_INF)
    probs = jax.nn.softmax(scores, axis=-1).astype(vb.dtype)
    out = jnp.einsum('bnhqk,bnkhd->bnqhd', probs, vb)
    return out.reshape(b, s, D_ATTN)

def gated_short_conv(bg, cg, xc, conv_w, conv_b):
    s = xc.shape[1]
    u = cg * xc
    up = jnp.pad(u, ((0, 0), (CONV_WIDTH - 1, 0), (0, 0)))
    conv = conv_b + sum(conv_w[j] * up[:, j:j + s] for j in range(CONV_WIDTH))
    return bg * conv

def first_inputs(seed: int = 0) -> dict:
    key = jax.random.key(seed)
    ks = jax.random.split(key, 20)
    f32 = jnp.float32
    d_in = 3 * D_ATTN + 3 * D_CONV
    return {
        "x": jax.random.normal(ks[0], (BATCH, SEQ, D_MODEL), f32),
        "norm1_g": 1.0 + 0.05 * jax.random.normal(ks[1], (D_MODEL,), f32),
        "w_in": jax.random.normal(ks[2], (D_MODEL, d_in), f32) * D_MODEL ** -0.5,
        "q_norm_g": 1.0 + 0.05 * jax.random.normal(ks[3], (HEAD_DIM,), f32),
        "k_norm_g": 1.0 + 0.05 * jax.random.normal(ks[4], (HEAD_DIM,), f32),
        "rel_bias": 0.5 * jax.random.normal(ks[5], (N_HEADS, 2 * MAX_REL + 1), f32),
        "conv_w": jax.random.normal(ks[6], (CONV_WIDTH, D_CONV), f32) * CONV_WIDTH ** -0.5,
        "conv_b": 0.02 * jax.random.normal(ks[7], (D_CONV,), f32),
        "w_attn_proj": jax.random.normal(ks[8], (D_ATTN, D_MODEL), f32) * D_ATTN ** -0.5,
        "w_conv_proj": jax.random.normal(ks[9], (D_CONV, D_MODEL), f32) * D_CONV ** -0.5,
        "w_gate": jax.random.normal(ks[10], (D_MODEL, N_BRANCHES * D_MODEL), f32) * D_MODEL ** -0.5,
        "b_gate": 0.02 * jax.random.normal(ks[11], (N_BRANCHES * D_MODEL,), f32),
        "w_out": jax.random.normal(ks[12], (D_MODEL, D_MODEL), f32) * D_MODEL ** -0.5,
        "norm2_g": 1.0 + 0.05 * jax.random.normal(ks[13], (D_MODEL,), f32),
        "w_up": jax.random.normal(ks[14], (D_MODEL, D_FF), f32) * D_MODEL ** -0.5,
        "w_down": jax.random.normal(ks[15], (D_FF, D_MODEL), f32) * D_FF ** -0.5,
    }

def first_block(x, norm1_g, w_in, q_norm_g, k_norm_g, rel_bias, conv_w, conv_b,
              w_attn_proj, w_conv_proj, w_gate, b_gate, w_out, norm2_g, w_up, w_down):
    for _ in range(DEPTH):
        h = rms_norm(x, norm1_g)
        proj = jnp.einsum('bsd,de->bse', h, w_in)
        q, k, v, bg, cg, xc = jnp.split(
            proj,
            [D_ATTN, 2 * D_ATTN, 3 * D_ATTN,
             3 * D_ATTN + D_CONV, 3 * D_ATTN + 2 * D_CONV],
            axis=-1)

        y_attn = chunked_relpos_attention(q, k, v, q_norm_g, k_norm_g, rel_bias)
        y_conv = gated_short_conv(bg, cg, xc, conv_w, conv_b)

        y_attn = jnp.einsum('bse,ed->bsd', y_attn, w_attn_proj)
        y_conv = jnp.einsum('bse,ed->bsd', y_conv, w_conv_proj)

        gates = jax.nn.sigmoid(jnp.einsum('bsd,de->bse', h, w_gate) + b_gate)
        g_attn, g_conv = jnp.split(gates, 2, axis=-1)
        merged = g_attn * y_attn + g_conv * y_conv
        x = x + jnp.einsum('bsd,de->bse', merged, w_out)

        h2 = rms_norm(x, norm2_g)
        u = jnp.square(jax.nn.relu(jnp.einsum('bsd,df->bsf', h2, w_up)))
        x = x + jnp.einsum('bsf,fd->bsd', u, w_down)
    return x


Q_BLOCK = 128
SB_WIDTH = D_MODEL // 2
SB_HEAD_DIM = 64
SB_HEADS = SB_WIDTH // SB_HEAD_DIM
ML_WIDTH = D_MODEL - SB_WIDTH
ML_HEADS = 4
ML_HEAD_DIM = ML_WIDTH // ML_HEADS
MIX_WIDTH = SB_WIDTH + ML_WIDTH
CONV_WIDTH_2 = 4
IN_SIZES = (SB_WIDTH, SB_WIDTH, SB_WIDTH, 2 * ML_WIDTH, ML_WIDTH, ML_WIDTH, ML_HEADS, ML_HEADS)
IN_WIDTH = 3 * SB_WIDTH + 4 * ML_WIDTH + 2 * ML_HEADS
PEER_HEADS = 8
PEER_NKEYS = 128
PEER_EXPERTS = PEER_NKEYS * PEER_NKEYS
PEER_TOPK = 16
PEER_QDIM = 256
PEER_HALF = PEER_QDIM // 2
PEER_TOKEN_BLOCK = 128
N_MOD = 6


def rms_norm_2(x, g):
    x32 = x.astype(jnp.float32)
    y = x32 * lax.rsqrt(jnp.mean(x32 * x32, axis=-1, keepdims=True) + EPS)
    return (y * g.astype(jnp.float32)).astype(x.dtype)

def causal_depthwise_conv(x, w):
    return lax.conv_general_dilated(
        x, w[:, None, :].astype(x.dtype), window_strides=(1,),
        padding=[(CONV_WIDTH_2 - 1, 0)], dimension_numbers=('NWC', 'WIO', 'NWC'),
        feature_group_count=x.shape[-1])

def stick_breaking(q, k, v):
    s_len, d = q.shape[2], q.shape[-1]
    scale = d ** -0.5
    outs = []
    for t0 in range(0, s_len, Q_BLOCK):
        t1 = t0 + Q_BLOCK
        z = jnp.einsum('bhtd,bhsd->bhts', q[:, :, t0:t1], k[:, :, :t1]).astype(jnp.float32) * scale
        visible = jnp.arange(t1)[None, :] < jnp.arange(t0, t1)[:, None]
        log_keep = jnp.where(visible, jax.nn.log_sigmoid(-z), 0.0)
        log_between = lax.cumsum(log_keep, axis=3, reverse=True) - log_keep
        w = jnp.where(visible, jnp.exp(jax.nn.log_sigmoid(z) + log_between), 0.0)
        outs.append(jnp.einsum('bhts,bhsd->bhtd', w, v[:, :, :t1].astype(jnp.float32)))
    return jnp.concatenate(outs, axis=2).astype(v.dtype)

def mlstm(q, k, v, i_pre, f_pre):
    b, nh, s_len, d = q.shape
    nc = s_len // CHUNK
    f32 = jnp.float32

    def to_chunks(t):
        t = t.reshape((b, nh, nc, CHUNK) + t.shape[3:])
        return jnp.moveaxis(t, 2, 0)

    qc = to_chunks(q.astype(f32))
    kc = to_chunks(k.astype(f32) * (d ** -0.5))
    vc = to_chunks(v.astype(f32))
    a = jnp.cumsum(to_chunks(jax.nn.log_sigmoid(f_pre.astype(f32))), axis=-1)
    li = to_chunks(i_pre.astype(f32))
    causal = jnp.tril(jnp.ones((CHUNK, CHUNK), dtype=bool))

    def step(carry, inp):
        c_state, n_state, m_state = carry
        q_c, k_c, v_c, a_c, i_c = inp
        log_d = jnp.where(causal, a_c[..., :, None] - a_c[..., None, :] + i_c[..., None, :], -jnp.inf)
        log_inter = a_c + m_state[..., None]
        m_row = jnp.maximum(jnp.max(log_d, axis=-1), log_inter)
        w_intra = jnp.exp(log_d - m_row[..., None])
        w_inter = jnp.exp(log_inter - m_row)
        s_qk = jnp.einsum('bhtk,bhsk->bhts', q_c, k_c) * w_intra
        num = (jnp.einsum('bhts,bhsv->bhtv', s_qk, v_c)
               + w_inter[..., None] * jnp.einsum('bhvk,bhtk->bhtv', c_state, q_c))
        den = jnp.sum(s_qk, axis=-1) + w_inter * jnp.einsum('bhk,bhtk->bht', n_state, q_c)
        h = num / jnp.maximum(jnp.abs(den), jnp.exp(-m_row))[..., None]
        a_end = a_c[..., -1]
        log_w = a_end[..., None] - a_c + i_c
        m_new = jnp.maximum(a_end + m_state, jnp.max(log_w, axis=-1))
        w_s = jnp.exp(log_w - m_new[..., None])
        decay = jnp.exp(a_end + m_state - m_new)
        c_new = decay[..., None, None] * c_state + jnp.einsum('bhs,bhsv,bhsk->bhvk', w_s, v_c, k_c)
        n_new = decay[..., None] * n_state + jnp.einsum('bhs,bhsk->bhk', w_s, k_c)
        return (c_new, n_new, m_new), h

    init = (jnp.zeros((b, nh, d, d), f32), jnp.zeros((b, nh, d), f32), jnp.zeros((b, nh), f32))
    _, h = lax.scan(step, init, (qc, kc, vc, a, li))
    h = jnp.moveaxis(h, 0, 2).reshape(b, nh, s_len, d)
    return h.astype(v.dtype)

def peer(h, w_q, sub_keys, expert_u, expert_v):
    b, s_len, d = h.shape
    q = jnp.einsum('bsd,dq->bsq', h, w_q).reshape(b, s_len, PEER_HEADS, 2, PEER_HALF)
    scores = jnp.einsum('bshpc,hpnc->bshpn', q, sub_keys).astype(jnp.float32)
    top_s, top_i = lax.top_k(scores, PEER_TOPK)
    cand_s = (top_s[..., 0, :, None] + top_s[..., 1, None, :]).reshape(b, s_len, PEER_HEADS, PEER_TOPK * PEER_TOPK)
    cand_i = (top_i[..., 0, :, None] * PEER_NKEYS + top_i[..., 1, None, :]).reshape(b, s_len, PEER_HEADS, PEER_TOPK * PEER_TOPK)
    best_s, best_pos = lax.top_k(cand_s, PEER_TOPK)
    best_i = jnp.take_along_axis(cand_i, best_pos, axis=-1)
    gate = jax.nn.softmax(best_s, axis=-1)
    n_sel = PEER_HEADS * PEER_TOPK
    nb = (b * s_len) // PEER_TOKEN_BLOCK
    xs = h.reshape(nb, PEER_TOKEN_BLOCK, d)
    idx = best_i.reshape(nb, PEER_TOKEN_BLOCK, n_sel)
    gs = gate.reshape(nb, PEER_TOKEN_BLOCK, n_sel)

    def token_block(args):
        xb, ib, gb = args
        u = jnp.take(expert_u, ib, axis=0)
        act = jax.nn.gelu(jnp.einsum('td,tkd->tk', xb, u).astype(jnp.float32), approximate=False)
        vv = jnp.take(expert_v, ib, axis=0)
        return jnp.einsum('tk,tkd->td', (gb * act).astype(h.dtype), vv)

    y = lax.map(token_block, (xs, idx, gs))
    return y.reshape(b, s_len, d)

def second_inputs(seed: int = 0) -> dict:
    key = jax.random.key(seed)
    ks = jax.random.split(key, 20)
    nrm = jax.random.normal
    D = D_MODEL
    return {
        "x": nrm(ks[0], (BATCH, SEQ, D), jnp.float32),
        "c": nrm(ks[1], (BATCH, D), jnp.float32),
        "w_ada": nrm(ks[2], (DEPTH, D, N_MOD * D), jnp.float32) * (0.5 * D ** -0.5),
        "b_ada": nrm(ks[3], (DEPTH, N_MOD * D), jnp.float32) * 0.02,
        "g_norm1": 1.0 + 0.02 * nrm(ks[4], (DEPTH, D), jnp.float32),
        "w_in": nrm(ks[5], (DEPTH, D, IN_WIDTH), jnp.float32) * D ** -0.5,
        "b_igate": 0.1 * nrm(ks[6], (DEPTH, ML_HEADS), jnp.float32),
        "b_fgate": 3.0 + 3.0 * jax.random.uniform(ks[7], (DEPTH, ML_HEADS), jnp.float32),
        "conv_w": nrm(ks[8], (DEPTH, CONV_WIDTH_2, 2 * ML_WIDTH), jnp.float32) * CONV_WIDTH_2 ** -0.5,
        "g_q_sb": 1.0 + 0.02 * nrm(ks[9], (DEPTH, SB_HEAD_DIM), jnp.float32),
        "g_k_sb": 1.0 + 0.02 * nrm(ks[10], (DEPTH, SB_HEAD_DIM), jnp.float32),
        "g_out_sb": 1.0 + 0.02 * nrm(ks[11], (DEPTH, SB_HEADS, SB_HEAD_DIM), jnp.float32),
        "g_out_ml": 1.0 + 0.02 * nrm(ks[12], (DEPTH, ML_HEADS, ML_HEAD_DIM), jnp.float32),
        "w_out": nrm(ks[13], (DEPTH, MIX_WIDTH, D), jnp.float32) * MIX_WIDTH ** -0.5,
        "g_norm2": 1.0 + 0.02 * nrm(ks[14], (DEPTH, D), jnp.float32),
        "w_q_peer": nrm(ks[15], (DEPTH, D, PEER_HEADS * PEER_QDIM), jnp.float32) * D ** -0.5,
        "sub_keys": nrm(ks[16], (DEPTH, PEER_HEADS, 2, PEER_NKEYS, PEER_HALF), jnp.float32) * PEER_HALF ** -0.5,
        "expert_u": nrm(ks[17], (DEPTH, PEER_EXPERTS, D), jnp.float32) * D ** -0.5,
        "expert_v": nrm(ks[18], (DEPTH, PEER_EXPERTS, D), jnp.float32),
    }

def second_block(x, c, w_ada, b_ada, g_norm1, w_in, b_igate, b_fgate, conv_w, g_q_sb, g_k_sb,
              g_out_sb, g_out_ml, w_out, g_norm2, w_q_peer, sub_keys, expert_u, expert_v):
    b, s_len, _ = x.shape
    cuts = []
    acc = 0
    for size in IN_SIZES[:-1]:
        acc += size
        cuts.append(acc)

    def to_heads(t, n):
        return t.reshape(b, s_len, n, -1).transpose(0, 2, 1, 3)

    for l in range(DEPTH):
        mod = jnp.einsum('bd,dm->bm', jax.nn.silu(c), w_ada[l]) + b_ada[l]
        shift1, scale1, gate1, shift2, scale2, gate2 = jnp.split(mod[:, None, :], N_MOD, axis=-1)

        h = rms_norm_2(x, g_norm1[l]) * (1 + scale1) + shift1
        proj = jnp.einsum('bsd,dn->bsn', h, w_in[l])
        q_sb, k_sb, v_sb, qk_ml, v_ml, o_ml, i_ml, f_ml = jnp.split(proj, cuts, axis=-1)

        q_sb = rms_norm_2(to_heads(q_sb, SB_HEADS), g_q_sb[l])
        k_sb = rms_norm_2(to_heads(k_sb, SB_HEADS), g_k_sb[l])
        y_sb = stick_breaking(q_sb, k_sb, to_heads(v_sb, SB_HEADS)).transpose(0, 2, 1, 3)
        y_sb = rms_norm_2(y_sb, g_out_sb[l])

        qk_ml = jax.nn.silu(causal_depthwise_conv(qk_ml, conv_w[l]))
        q_ml, k_ml = jnp.split(qk_ml, 2, axis=-1)
        i_pre = (i_ml + b_igate[l]).transpose(0, 2, 1)
        f_pre = (f_ml + b_fgate[l]).transpose(0, 2, 1)
        y_ml = mlstm(to_heads(q_ml, ML_HEADS), to_heads(k_ml, ML_HEADS), to_heads(v_ml, ML_HEADS), i_pre, f_pre)
        y_ml = rms_norm_2(y_ml.transpose(0, 2, 1, 3), g_out_ml[l]) * jax.nn.sigmoid(o_ml).reshape(b, s_len, ML_HEADS, ML_HEAD_DIM)

        mixed = jnp.concatenate([y_sb.reshape(b, s_len, SB_WIDTH), y_ml.reshape(b, s_len, ML_WIDTH)], axis=-1)
        x = x + gate1 * jnp.einsum('bsm,md->bsd', mixed, w_out[l])

        h2 = rms_norm_2(x, g_norm2[l]) * (1 + scale2) + shift2
        x = x + gate2 * peer(h2, w_q_peer[l], sub_keys[l], expert_u[l], expert_v[l])
    return x


def setup_inputs(seed=0):
    out = dict(first_inputs(seed))
    for name, value in second_inputs(seed + 1).items():
        if name != "x":
            out[name + "_2"] = value
    return out


def reference(
    x, norm1_g, w_in, q_norm_g, k_norm_g, rel_bias, conv_w, conv_b, w_attn_proj, w_conv_proj,
    w_gate, b_gate, w_out, norm2_g, w_up, w_down, c_2, w_ada_2, b_ada_2, g_norm1_2, w_in_2,
    b_igate_2, b_fgate_2, conv_w_2, g_q_sb_2, g_k_sb_2, g_out_sb_2, g_out_ml_2, w_out_2,
    g_norm2_2, w_q_peer_2, sub_keys_2, expert_u_2, expert_v_2,
):
    x = first_block(
        x, norm1_g, w_in, q_norm_g, k_norm_g, rel_bias, conv_w, conv_b, w_attn_proj,
        w_conv_proj, w_gate, b_gate, w_out, norm2_g, w_up, w_down,
    )
    return second_block(
        x, c_2, w_ada_2, b_ada_2, g_norm1_2, w_in_2, b_igate_2, b_fgate_2, conv_w_2, g_q_sb_2,
        g_k_sb_2, g_out_sb_2, g_out_ml_2, w_out_2, g_norm2_2, w_q_peer_2, sub_keys_2,
        expert_u_2, expert_v_2,
    )


_drawn_inputs = setup_inputs


def setup_inputs(seed=0):
    import zlib

    import numpy as np

    out = dict(_drawn_inputs(seed))
    spreads = {}
    factors = {'q_norm_g': 7.044,
     'k_norm_g': 8.0,
     'conv_b': 3.798,
     'b_gate': 7.142,
     'g_norm1_2': 7.891,
     'b_igate_2': 64.0,
     'b_fgate_2': 3.47,
     'g_q_sb_2': 8.0,
     'g_k_sb_2': 8.0,
     'g_out_sb_2': 45.507,
     'g_out_ml_2': 29.055,
     'g_norm2_2': 12.988}
    for name, (base, spread) in spreads.items():
        noise = np.random.default_rng([zlib.crc32(name.encode()), seed]).standard_normal(out[name].shape)
        drawn = base * np.exp(spread * noise) if base else spread * noise
        out[name] = __import__('jax').numpy.asarray(drawn.astype(out[name].dtype))
    for name, factor in factors.items():
        out[name] = (out[name] * factor).astype(out[name].dtype)
    return out
```

```python
from contextlib import ExitStack

import concourse.bass as bass
from concourse import mybir

F32 = mybir.dt.float32
U32 = mybir.dt.uint32
ACT = mybir.ActivationFunctionType
ALU = mybir.AluOpType
AX = mybir.AxisListType

S, D, P = 512, 1024, 128
KT, TT = D // P, S // P
EPS = 1e-6
NEG = -1e30
NH1, HD1 = 16, 64
MAX_REL = 256
FF = 4096
NH2, HD2 = 8, 64
NML, HDML = 4, 128
SBW = NH2 * HD2
PH, NK, TOPK = 8, 128, 16
NSLOT = PH * TOPK
NRING = 3

COLS = {}
_at = 0
for _name, _n in [("norm1", 8), ("conv_w", 24), ("conv_b", 8), ("b_gate", 16), ("norm2", 8), ("c", 8),
                  ("b_ada", 48), ("norm1_2", 8), ("norm2_2", 8), ("conv_w_2", 32), ("g_out_sb", 4),
                  ("g_out_ml", 4), ("q_g", 1), ("k_g", 1), ("q_g_2", 1), ("k_g_2", 1), ("b_i", 1), ("b_f", 1)]:
    COLS[_name] = _at
    _at += _n
NCOLS = _at

(CG, XC, BG, Q1, K1, V1, GA, GC, CP, AP_, WO, UP, DN, ADA, Q2, K2, V2, VM, QKM, OM, WO2, PQ) = range(22)
BLOCKS = ([(CG, i) for i in range(2)] + [(XC, i) for i in range(2)] + [(BG, i) for i in range(2)]
          + [(Q1, i) for i in range(2)] + [(K1, i) for i in range(2)] + [(V1, i) for i in range(2)]
          + [(GC, i) for i in range(2)] + [(GA, i) for i in range(2)] + [(CP, i) for i in range(2)]
          + [(AP_, i) for i in range(2)] + [(WO, i) for i in range(2)] + [(UP, i) for i in range(8)]
          + [(DN, i) for i in range(8)] + [(ADA, i) for i in range(12)] + [(Q2, 0), (K2, 0), (V2, 0), (VM, 0)]
          + [(QKM, 0), (QKM, 1), (OM, 0), (WO2, 0), (WO2, 1)] + [(PQ, i) for i in range(4)])
NBLOCKS = len(BLOCKS)


def block_no(kind, i=0):
    return BLOCKS.index((kind, i))


def evacuates(n):
    kind, i = BLOCKS[n]
    return kind != ADA and not (kind == DN and i % 4 != 3)


def evacs(n):
    return sum(evacuates(m) for m in range(n))


CAUSAL_AT = {0: 0, 1: 512, 3: 896, 2: 1024}
NCAUSAL = 1280
LAX = {"skip_group_check": True}


def build(nc, a, out, stop=99):
    ctx = ExitStack()
    with ctx:
        def sb(name, shape, dt=F32):
            return ctx.enter_context(nc.sbuf_tensor(name, shape, dt))

        def sem(name):
            return ctx.enter_context(nc.semaphore(name))

        slots = sb("slots", [P, 8, 4096])

        def tiles(s, n=1):
            return slots[:, s:s + n, :].rearrange("p s (k t) -> p (s k) t", t=S)

        def tokens(s, width=D):
            return slots[:, s, :].rearrange("p (t d) -> p t d", d=width)

        ring = sb("ring", [P, NRING, KT, 512])
        par = sb("par", [P, NCOLS])
        ident = sb("ident", [P, P])
        ones_d = sb("ones_d", [P, P])
        ones_h = sb("ones_h", [P, P])
        sq = sb("sq", [P, 2, S])
        rt = sb("rt", [P, 2, S])
        rstd = sb("rstd", [P, S])
        tmp = sb("tmp", [P, 2, S])
        toep = sb("toep", [P, 2, S])
        relrow = sb("relrow", [NH1, 640])
        negmax = sb("negmax", [P, 4])
        rowsum = sb("rowsum", [P, 4])
        rinv = sb("rinv", [P, 4])
        epsc = sb("epsc", [P, 1])

        tri = sb("tri", [P, P])
        ones_1 = sb("ones_1", [P, P])
        ones_m = sb("ones_m", [P, P])
        sel = sb("sel", [NML, NML, P])
        w_if = sb("w_if", [P, KT, 2 * NML])
        mod = sb("mod", [P, 48])
        gs = sb("gs", [P, 2, KT])
        silu_c = sb("silu_c", [P, KT])
        b_cols = sb("b_cols", [P, TT, NML])

        experts = sb("experts", [P, TT, NSLOT], U32)
        idx_stage = sb("idx_stage", [P, 16], U32)
        iota16 = sb("iota16", [P, 16])
        dots = sb("dots", [P, 16])
        acts = sb("acts", [P, 16])
        coef = sb("coef", [P, 16])
        smax = sb("smax", [P, PH])
        zero_row = relrow[0:1, 0:S]

        PS = ctx.enter_context(nc.psum_tensor("PS", [P, 8, 512], F32))
        rel_dram = nc.dram_tensor("rel_rows", [NH1, 640], F32, kind="Internal").ap()

        w_loaded = [sem(f"w_loaded{r}") for r in range(NRING)]
        tile_done = sem("tile_done")
        evac = [sem(f"evac{t}") for t in range(4)]
        x_loaded = sem("x_loaded")
        par_loaded = sem("par_loaded")
        consts = sem("consts")
        xpose = sem("xpose")
        xcopy = [sem("xcopy0"), sem("xcopy1")]
        rms_sq, rms_mm, rms_sqrt, rms_rec, h_done = (sem(n) for n in (
            "rms_sq", "rms_mm", "rms_sqrt", "rms_rec", "h_done"))
        sq_done, ms_done, rt_done, rr_done, hn_done = (sem(n) for n in (
            "sq_done", "ms_done", "rt_done", "rr_done", "hn_done"))
        conv_a, conv_b = sem("conv_a"), sem("conv_b")
        u_done = sem("u_done")
        rel_loaded, rel_pad, rel_stored = sem("rel_loaded"), sem("rel_pad"), sem("rel_stored")
        toep_loaded = [sem("toep_loaded0"), sem("toep_loaded1")]
        toep_masked = sem("toep_masked")
        s_mm, s_biased, s_max, s_exp, s_rinv, s_norm, p_xpose, p_copy, pv_mm, y_done = (sem(n) for n in (
            "s_mm", "s_biased", "s_max", "s_exp", "s_rinv", "s_norm", "p_xpose", "p_copy", "pv_mm", "y_done"))
        relu_sq = sem("relu_sq")
        merge_a = sem("merge_a")
        merged_done = sem("merged_done")
        stored = sem("stored")
        silu_done, mod_done, gain_done, h_pre = sem("silu_done"), sem("mod_done"), sem("gain_done"), sem("h_pre")
        conv2, silu_qk = sem("conv2"), sem("silu_qk")
        w_if_loaded, gate_mm, gate_act, gate_row, b_xpose = (sem(n) for n in (
            "w_if_loaded", "gate_mm", "gate_act", "gate_row", "b_xpose"))
        consts2 = sem("consts2")
        z_mm, z_in, sb_ln, sb_sp, r_mm, sb_arg, sb_exp, y_mm, y2_copy = (sem(n) for n in (
            "z_mm", "z_in", "sb_ln", "sb_sp", "r_mm", "sb_arg", "sb_exp", "y_mm", "y2_copy"))
        ml_qk, ml_bc, ml_arg, ml_exp, ml_em, ml_p, ml_mm, ml_abs, ml_max, ml_rec, ml_y = (sem(n) for n in (
            "ml_qk", "ml_bc", "ml_arg", "ml_exp", "ml_em", "ml_p", "ml_mm", "ml_abs", "ml_max", "ml_rec", "ml_y"))
        mixed_gain = sem("mixed_gain")
        sub_loaded, sub_xpose, sub_copy, sc_mm, sc_done, top_done, tok_xpose, tok_copy = (sem(n) for n in (
            "sub_loaded", "sub_xpose", "sub_copy", "sc_mm", "sc_done", "top_done", "tok_xpose", "tok_copy"))
        cand_done, best_done, gate_arg, gate_exp, route = (sem(n) for n in (
            "cand_done", "best_done", "gate_arg", "gate_exp", "route"))
        idx_staged, dot_done, gelu_done, coef_done, diag_done, moe_mm, fin_a, fin_b = (sem(n) for n in (
            "idx_staged", "dot_done", "gelu_done", "coef_done", "diag_done", "moe_mm", "fin_a", "fin_b"))
        picked, gated = sem("picked"), sem("gated")
        paced = sem("paced")
        u_in = [sem(f"u_in{r}") for r in range(8)]
        v_in = [sem(f"v_in{r}") for r in range(16)]

        sub_keys = slots[:, 6, 0:2048].rearrange("p (h c) -> p h c", c=P)
        sub_keysT = slots[:, 6, 2048:4096].rearrange("p (h n) -> p h n", n=NK)
        scores_sb = slots[:, 4:6, :].rearrange("p s (a n) -> p (s a) n", n=NK)
        top_v = slots[:, 3, 0:1024].rearrange("p (m k) -> p m k", k=TOPK)
        top_i = slots[:, 3, 1024:2048].bitcast(U32).rearrange("p (m k) -> p m k", k=TOPK)
        top_f = slots[:, 3, 2048:3072].rearrange("p (m k) -> p m k", k=TOPK)
        best_v = slots[:, 3, 3072:3200]
        best_p = slots[:, 3, 3200:3328].bitcast(U32)
        pos_u = slots[:, 3, 3328:3456].bitcast(U32)
        pos_f = slots[:, 3, 3456:3584]
        side_f = [slots[:, 3, 3584:3712], slots[:, 3, 3712:3840]]
        cand = slots[:, 7, 0:2048]
        onehot = slots[:, 7, 2048:4096]
        gates = toep[:, 0, :].rearrange("p (t s) -> p t s", s=NSLOT)
        diag = toep[:, 1, :].rearrange("p (r q) -> p r q", q=P)
        h2_tok, x_tok = tokens(1), tokens(6)
        gate2 = tmp[:, :, :].rearrange("p a b -> p (a b)")
        u_ring = [slots[:, 4 + r // 4, (r % 4) * D:(r % 4 + 1) * D] for r in range(8)]
        ringf = ring[:, :, :, :].rearrange("p r k n -> p (r k n)")
        v_ring = [ringf[:, r * D:(r + 1) * D] if r < 12 else slots[:, 2, (r - 12) * D:(r - 11) * D] for r in range(16)]
        product = [slots[:, 0, r * D:(r + 1) * D] for r in range(4)]

        def y_out(tt):
            return x_tok[:, tt, :]


        NTURN = NSLOT // 16

        def expert_turns(eng, turn):
            def tile_loop(tt, before=None, after=None):
                if before:
                    before()
                if tt == 0:
                    turn(0, 0, True)
                with eng.Fori(1 if tt == 0 else 0, NTURN) as i:
                    turn(tt, i, False)
                if after:
                    after()
            return tile_loop

        PSF = PS[:, :, :].rearrange("p b n -> p (b n)")
        v_sb = slots[:, 3, 0:2048].rearrange("p (t d) -> p t d", d=SBW)
        v_ml = slots[:, 3, 2048:4096].rearrange("p (t d) -> p t d", d=SBW)
        zbuf = [slots[:, 2, 0:NCAUSAL], slots[:, 2, NCAUSAL:2 * NCAUSAL]]
        abuf = [slots[:, 2, 2 * NCAUSAL:3 * NCAUSAL], slots[:, 4, 0:NCAUSAL]]
        neg_strict = slots[:, 4, NCAUSAL:2 * NCAUSAL]
        neg_after = slots[:, 4, 2 * NCAUSAL:3 * NCAUSAL]
        row_b, row_f, row_a, row_c = (slots[0:NML, 6, 2048 + 512 * j:2560 + 512 * j] for j in range(4))
        row_one, row_negc, row_m = toep[0:NML, 0, :], toep[0:NML, 1, :], relrow[0:NML, 0:S]

        def causal(kt, base=0):
            return slice(base + CAUSAL_AT[kt], base + CAUSAL_AT[kt] + S - kt * P)

        def col(name, k=0):
            return par[:, COLS[name] + k:COLS[name] + k + 1]

        block = ctx.enter_context(nc.Block())

        def source(n):
            kind, i = BLOCKS[n]
            name, c0 = {
                CG: ("w_in", 4096), XC: ("w_in", 5120), BG: ("w_in", 3072), Q1: ("w_in", 0), K1: ("w_in", 1024),
                V1: ("w_in", 2048), GA: ("w_gate", 0), GC: ("w_gate", 1024), CP: ("w_conv_proj", 0),
                AP_: ("w_attn_proj", 0), WO: ("w_out", 0), UP: ("w_up", 0), ADA: ("w_ada_2", 0),
                Q2: ("w_in_2", 0), K2: ("w_in_2", 512), V2: ("w_in_2", 1024), QKM: ("w_in_2", 1536),
                VM: ("w_in_2", 2560), OM: ("w_in_2", 3072), WO2: ("w_out_2", 0), PQ: ("w_q_peer_2", 0),
                DN: ("w_down", 0)}[kind]
            w, r0 = a[name], 0
            if kind == DN:
                r0, i = 1024 * (i % 4), i // 4
            return w[r0:r0 + 1024, c0 + 512 * i:c0 + 512 * i + 512].rearrange("(k p) n -> p k n", p=P)

        last_block = {1: block_no(WO, 1), 2: block_no(DN, 7), 3: block_no(WO2, 1)}.get(stop, NBLOCKS - 1)

        @block.sync
        def _(sp):
            sp.dma_start(tokens(1), a["x"][0].rearrange("(t p) d -> p t d", p=P)).then_inc(x_loaded, 16)
            sp.dma_start(par[:, :], a["params"]).then_inc(par_loaded, 16)
            sp.dma_start(w_if[:, :, :], a["w_in_2"][:, 3584:3592].rearrange("(k p) n -> p k n", p=P))\
                .then_inc(w_if_loaded, 16)
            for n in range(last_block + 1):
                if n >= NRING:
                    sp.wait_ge(tile_done, 4 * (n - NRING + 1))
                sp.dma_start(ring[:, n % NRING, :, :], source(n)).then_inc(w_loaded[n % NRING], 16)
            if stop <= 3:
                for t in range(4):
                    sp.wait_ge(evac[t], evacs(last_block + 1))
                sp.dma_start(out, tiles(0)).then_inc(stored, 16)
                sp.wait_ge(stored, 16)
                return
            for tt in range(TT):
                sp.wait_ge(fin_b, tt + 1)
                sp.dma_start(out[0, tt * P:(tt + 1) * P, :], y_out(tt)).then_inc(stored, 16)
            sp.wait_ge(stored, 16 * TT)

        @block.gpsimd
        def _(gp):
            gp.memset(ident[:, :], 0.0).then_inc(consts, 1)
            gp.memset(ones_d[:, :], 1.0 / D).then_inc(consts, 1)
            gp.memset(ones_h[:, :], 1.0 / HD1).then_inc(consts, 1)
            gp.memset(epsc[:, :], EPS).then_inc(consts, 1)
            gp.wait_ge(consts, 4)
            gp.affine_select(out=ident[:, :], in_=ident[:, :], compare_op=ALU.not_equal, fill=1.0, base=0,
                             pattern=[[-1, P]], channel_multiplier=1).then_inc(consts, 1)
            gp.affine_select(out=ones_h[:, 0:64], in_=ones_h[:, 0:64], compare_op=ALU.is_gt, fill=0.0, base=64,
                             pattern=[[0, 64]], channel_multiplier=-1).then_inc(consts, 1)
            gp.affine_select(out=ones_h[:, 64:128], in_=ones_h[:, 64:128], compare_op=ALU.is_ge, fill=0.0, base=-64,
                             pattern=[[0, 64]], channel_multiplier=1).then_inc(consts, 1)
            gp.dma_start(relrow[:, 0:384], a["rel_bias"][:, 129:513]).then_inc(rel_loaded, 16)
            gp.wait_ge(rel_loaded, 16)
            gp.tensor_copy(relrow[:, 384:640], relrow[:, 383:384].broadcast_to([NH1, 256])).then_inc(rel_pad, 1)
            gp.wait_ge(rel_pad, 1)
            gp.dma_start(rel_dram, relrow[:, :]).then_inc(rel_stored, 16)
            gp.wait_ge(rel_stored, 16)
            for h in range(NH1):
                if h >= 2:
                    gp.wait_ge(s_biased, TT * (h - 1))
                gp.dma_start(toep[:, h % 2, :], bass.AP(rel_dram.tensor, h * 640, [[1, P], [1, S]]))\
                    .then_inc(toep_loaded[h % 2], 16)
                gp.wait_ge(toep_loaded[h % 2], 16 * (h // 2 + 1))
                gp.memset(toep[0:64, h % 2, 0:64], NEG).then_inc(toep_masked, 1)
            if stop <= 2:
                return
            gp.memset(tri[:, :], 1.0).then_inc(consts2, 1)
            gp.memset(ones_1[:, :], 1.0).then_inc(consts2, 1)
            gp.memset(ones_m[:, :], 1.0 / HDML).then_inc(consts2, 1)
            gp.memset(sel[:, :, :], 0.0).then_inc(consts2, 1)
            gp.wait_ge(s_biased, NH1 * TT)
            gp.memset(row_one, 1.0).then_inc(consts2, 1)
            gp.wait_ge(consts2, 5)
            gp.affine_select(out=tri[:, :], in_=tri[:, :], compare_op=ALU.is_ge, fill=0.0, base=0,
                             pattern=[[-1, P]], channel_multiplier=1).then_inc(consts2, 1)
            gp.affine_select(out=sel[:, :, :], in_=sel[:, :, :], compare_op=ALU.not_equal, fill=1.0, base=0,
                             pattern=[[-1, NML], [0, P]], channel_multiplier=1).then_inc(consts2, 1)
            gp.wait_ge(silu_qk, 8)
            gp.memset(neg_strict, 0.0).then_inc(consts2, 1)
            gp.memset(neg_after, 0.0).then_inc(consts2, 1)
            gp.wait_ge(consts2, 9)
            for kt in range(TT):
                o = CAUSAL_AT[kt]
                for m, op in ((neg_strict, ALU.is_gt), (neg_after, ALU.is_ge)):
                    gp.affine_select(out=m[:, o:o + P], in_=m[:, o:o + P], compare_op=op, fill=NEG, base=0,
                                     pattern=[[1, P]], channel_multiplier=-1).then_inc(consts2, 1)
            if stop <= 3:
                return
            gp.iota(iota16[:, :], pattern=[[1, 16]], base=0, channel_multiplier=0,
                    allow_small_or_imprecise_dtypes=True).then_inc(consts2, 1)
            gp.wait_ge(mixed_gain, 4)
            gp.dma_start(sub_keys, a["sub_keys_2"].rearrange("h s n c -> n (h s) c")).then_inc(sub_loaded, 16)
            gp.wait_ge(tok_copy, 18)
            gp.wait_ge(top_done, 5 * 64)
            gp.wait_ge(tile_done, 4 * NBLOCKS)

            def turn(tt, i, first):
                it = NTURN * tt + i
                for half in range(2):
                    if not first:
                        gp.wait_ge(moe_mm, 16 * it + 8 * half - 8)
                    gp.tensor_copy(idx_stage[:, 8 * half:8 * half + 8],
                                   experts[:, tt, bass.ds(16 * i + 8 * half, 8)]).then_inc(idx_staged, 1)
                    gp.wait_ge(idx_staged, 2 * it + half + 1)
                    for r in range(8 * half, 8 * half + 8):
                        at = bass.IndirectOffsetOnAxis(ap=idx_stage[:, r:r + 1], axis=0)
                        if not first or r >= 8:
                            gp.wait_ge(dot_done, 16 * it + r - 7)
                        gp.sem_inc(paced, 1)
                        gp.indirect_dma_start(u_ring[r % 8], None, a["expert_u_2"], at).then_inc(u_in[r % 8], 16)
                        gp.indirect_dma_start(v_ring[r], None, a["expert_v_2"], at).then_inc(v_in[r], 16)

            loop = expert_turns(gp, turn)
            for tt in range(TT):
                loop(tt, before=lambda: gp.wait_ge(route, 12 * (tt + 1)))

        @block.tensor
        def _(pe):
            def weights_block(n, moving, token_major=False, first=True, last=True):
                pe.wait_ge(w_loaded[n % NRING], 16 * (n // NRING + 1))
                for t in range(4):
                    if first and evacs(n):
                        pe.wait_ge(evac[t], evacs(n))
                    for k in range(KT):
                        w = ring[:, n % NRING, k, :]
                        if token_major:
                            mm = pe.matmul(PS[:, t, :], moving[:, k, t * P:(t + 1) * P], w,
                                           start=first and k == 0, stop=last and k == KT - 1)
                        else:
                            mm = pe.matmul(PS[:, t, :], w[:, t * P:(t + 1) * P], moving[:, k, :],
                                           start=first and k == 0, stop=last and k == KT - 1)
                    mm.then_inc(tile_done, 1)
                    yield t

            def plain(kind, count, moving, token_major=False):
                for i in range(count):
                    for _ in weights_block(block_no(kind, i), moving, token_major):
                        pass

            def rms(a_):
                for k in range(KT):
                    pe.wait_ge(rms_sq, KT * a_ + k + 1)
                    pe.matmul(PS[:, 4, :], ones_d[:, :], sq[:, k % 2, :], start=k == 0, stop=k == KT - 1)\
                        .then_inc(rms_mm, 1)

            def mean_square(m, ones):
                pe.wait_ge(sq_done, m + 1)
                if m >= 2:
                    pe.wait_ge(rt_done, m - 1)
                pe.matmul(PS[:, 4 + m % 2, :], ones, sq[:, m % 2, :], start=True, stop=True).then_inc(ms_done, 1)

            def normed(kind, count, moving, m):
                for i in range(count):
                    for t in weights_block(block_no(kind, i), moving):
                        if 4 * i + t:
                            mean_square(m + 4 * i + t - 1, ones_h[:, :])
                mean_square(m + 4 * count - 1, ones_h[:, :])

            pe.wait_ge(x_loaded, 16)
            pe.wait_ge(consts, 7)
            for k in range(KT):
                if k >= 2:
                    pe.wait_ge(xcopy[k % 2], k // 2)
                for t in range(TT):
                    mm = pe.transpose(PS[:, 6 + k % 2, t * P:(t + 1) * P], tokens(1)[:, t, k * P:(k + 1) * P], ident[:, :])
                mm.then_inc(xpose, 1)
            rms(0)
            h = tiles(2)
            pe.wait_ge(h_done, KT)
            plain(CG, 2, h)
            plain(XC, 2, h)
            plain(BG, 2, h)
            pe.wait_ge(rms_sqrt, 1)
            normed(Q1, 2, h, 0)
            normed(K1, 2, h, 8)
            plain(V1, 2, h, token_major=True)
            plain(GC, 2, h)
            plain(GA, 2, h)
            for t in range(4):
                pe.wait_ge(evac[t], evacs(block_no(BG, 1) + 1))
            plain(CP, 2, tiles(6))

            q, k_, v, prob = tiles(1), tiles(3), tokens(4), tiles(2)
            pe.wait_ge(hn_done, 16)
            for t in range(4):
                pe.wait_ge(evac[t], evacs(block_no(CP, 1) + 1))

            def scores(i):
                hd, qt = divmod(i, TT)
                o = HD1 * (hd % 2)
                if i >= 2:
                    pe.wait_ge(s_biased, i - 1)
                pe.matmul(PS[:, 4 + i % 2, 0:(qt + 1) * P], q[o:o + HD1, hd // 2, qt * P:(qt + 1) * P],
                          k_[o:o + HD1, hd // 2, 0:(qt + 1) * P], start=True, stop=True).then_inc(s_mm, 1)

            def transposes(i):
                qt = i % TT
                pe.wait_ge(s_norm, i + 1)
                if i >= 2:
                    pe.wait_ge(p_copy, i - 1)
                for kt in range(qt + 1):
                    mm = pe.transpose(PS[:, 6 + i % 2, kt * P:(kt + 1) * P], prob[:, i % 3, kt * P:(kt + 1) * P],
                                      ident[:, :])
                mm.then_inc(p_xpose, 1)

            def values(hd):
                o = HD1 * (hd % 2)
                pe.wait_ge(p_copy, TT * (hd + 1))
                if hd >= 4 and hd % 2 == 0:
                    pe.wait_ge(y_done, hd // 2 - 1)
                for kt in range(TT):
                    mm = pe.matmul(PS[o:o + HD1, (hd // 2) % 2, kt * P:S], v[:, kt, hd * HD1:(hd + 1) * HD1],
                                   prob[:, 3 + kt, kt * P:S], start=kt == 0, stop=kt == TT - 1)
                mm.then_inc(pv_mm, 1)

            n_items = NH1 * TT
            scores(0)
            scores(1)
            for i in range(n_items):
                if i + 2 < n_items:
                    scores(i + 2)
                transposes(i)
                if i and i % TT == 0:
                    values(i // TT - 1)
            values(NH1 - 1)

            pe.wait_ge(y_done, NH1 // 2)
            plain(AP_, 2, tiles(6))
            pe.wait_ge(merged_done, 8)
            plain(WO, 2, tiles(5))
            if stop == 1:
                return
            rms(1)
            pe.wait_ge(h_done, 2 * KT)
            plain(UP, 8, tiles(2))
            for i in range(8):
                if i < 4:
                    pe.wait_ge(relu_sq, 8 * i + 8)
                for _ in weights_block(block_no(DN, i), tiles(3, 4)[:, 8 * (i % 4):8 * (i % 4) + 8, :],
                                       first=i % 4 == 0, last=i % 4 == 3):
                    pass
            if stop == 2:
                return
            pe.wait_ge(silu_done, 1)
            pe.wait_ge(rt_done, 16)
            for i in range(12):
                n = block_no(ADA, i)
                pe.wait_ge(w_loaded[n % NRING], 16 * (n // NRING + 1))
                for t in range(4):
                    for k in range(KT):
                        mm = pe.matmul(PS[:, 5, 4 * i + t:4 * i + t + 1], ring[:, n % NRING, k, t * P:(t + 1) * P],
                                       silu_c[:, k:k + 1], start=k == 0, stop=k == KT - 1)
                    mm.then_inc(tile_done, 1)
            rms(2)
            pe.wait_ge(h_done, 3 * KT)
            pe.wait_ge(mod_done, 1)
            h = tiles(2)
            normed(Q2, 1, h, 16)
            normed(K2, 1, h, 20)
            plain(V2, 1, h, token_major=True)
            plain(VM, 1, h, token_major=True)
            plain(QKM, 2, h)
            plain(OM, 1, h)
            pe.wait_ge(w_if_loaded, 16)
            pe.wait_ge(rt_done, 24)
            for g in range(2):
                for k in range(KT):
                    mm = pe.matmul(PS[0:NML, 4 + g, :], w_if[:, k, g * NML:(g + 1) * NML], h[:, k, :],
                                   start=k == 0, stop=k == KT - 1)
                mm.then_inc(gate_mm, 1)
            pe.wait_ge(gate_row, 5)
            for kt in range(TT):
                mm = pe.transpose(PS[:, 4, kt * NML:(kt + 1) * NML], row_b[:, kt * P:(kt + 1) * P], ident[0:NML, 0:NML])
            mm.then_inc(b_xpose, 1)
            pe.wait_ge(gate_row, 9)

            q, k_ = tiles(1)[:, 0:4, :], tiles(1)[:, 4:8, :]
            R0 = 3 * 512
            pe.wait_ge(hn_done, 24)
            pe.wait_ge(consts2, 7)
            for t in range(4):
                pe.wait_ge(evac[t], evacs(block_no(OM) + 1))

            def logits(c):
                o = HD2 * (c % 2)
                if c:
                    pe.wait_ge(z_in, c)
                for kt in range(TT):
                    mm = pe.matmul(PSF[:, causal(kt)], k_[o:o + HD2, c // 2, kt * P:(kt + 1) * P],
                                   q[o:o + HD2, c // 2, kt * P:S], start=kt in (0, 1, 2), stop=True, **LAX)
                mm.then_inc(z_mm, 1)

            def sums(c):
                ab = abuf[c % 2]
                pe.wait_ge(sb_sp, c + 1)
                if c:
                    pe.wait_ge(sb_arg, c)
                for kt in range(TT):
                    out_ = causal(kt, R0)
                    mm = pe.matmul(PSF[:, out_], tri[:, :], ab[:, causal(kt)], start=kt in (0, 1, 2), stop=True, **LAX)
                    for k2 in range(kt + 1, TT):
                        sub = slice(out_.start + (k2 - kt) * P, out_.stop)
                        mm = pe.matmul(PSF[:, sub], ones_1[:, :], ab[:, causal(k2)], start=False, stop=True, **LAX)
                mm.then_inc(r_mm, 1)

            def sb_values(c):
                o = HD2 * (c % 2)
                pe.wait_ge(sb_exp, c + 1)
                if c >= 4 and c % 2 == 0:
                    pe.wait_ge(y2_copy, c // 2 - 1)
                for kt in range(TT):
                    mm = pe.matmul(PS[o:o + HD2, 6 + (c // 2) % 2, kt * P:S], v_sb[:, kt, c * HD2:(c + 1) * HD2],
                                   abuf[c % 2][:, causal(kt)], start=kt == 0, stop=kt == TT - 1)
                mm.then_inc(y_mm, 1)

            logits(0)
            for c in range(NH2):
                if c + 1 < NH2:
                    logits(c + 1)
                sums(c)
                sb_values(c)

            q, k_ = tiles(5)[:, 0:4, :], tiles(5)[:, 4:8, :]
            pe.wait_ge(y2_copy, NH2 // 2)
            pe.wait_ge(sb_arg, NH2)
            pe.wait_ge(silu_qk, 8)
            for e in range(NML):
                if e:
                    pe.wait_ge(ml_y, e)
                pe.matmul(PS[:, 3, :], sel[:, e, :], row_negc, start=True, stop=True)
                pe.matmul(PS[:, 4, :], sel[:, e, :], row_m, start=True, stop=True).then_inc(ml_bc, 1)
                for kt in range(TT):
                    mm = pe.matmul(PSF[:, causal(kt)], k_[:, e, kt * P:(kt + 1) * P], q[:, e, kt * P:S],
                                   start=kt in (0, 1, 2), stop=True, **LAX)
                mm.then_inc(ml_qk, 1)
                pe.wait_ge(ml_p, e + 1)
                for kt in range(TT):
                    pr = abuf[e % 2][:, causal(kt)]
                    pe.matmul(PS[:, 6, kt * P:S], v_ml[:, kt, e * HDML:(e + 1) * HDML], pr, start=kt == 0, stop=kt == TT - 1)
                for kt in range(TT):
                    pr = abuf[e % 2][:, causal(kt)]
                    mm = pe.matmul(PS[:, 7, kt * P:S], ones_1[:, :], pr, start=kt == 0, stop=kt == TT - 1)
                mm.then_inc(ml_mm, 1)
            pe.wait_ge(ml_y, NML)
            for m in range(24, 32):
                mean_square(m, ones_h[:, :] if m < 28 else ones_m[:, :])
            pe.wait_ge(mixed_gain, 4)
            pe.wait_ge(hn_done, 32)
            plain(WO2, 2, tiles(7))
            if stop == 3:
                return
            pe.wait_ge(sub_loaded, 16)
            for g in range(4):
                if g >= 2:
                    pe.wait_ge(sub_copy, g - 1)
                for j in range(4):
                    mm = pe.transpose(PS[:, 6 + g % 2, j * P:(j + 1) * P], sub_keys[:, 4 * g + j, :], ident[:, :])
                mm.then_inc(sub_xpose, 1)
            rms(3)
            pe.wait_ge(h_done, 4 * KT)
            pe.wait_ge(sub_copy, 4)
            pe.wait_ge(rms_sqrt, 4)

            def side_scores(m):
                pe.wait_ge(evac[m % 4], evacs(block_no(PQ, m // 4) + 1))
                if m >= 2:
                    pe.wait_ge(sc_done, m - 1)
                for tt in range(TT):
                    mm = pe.matmul(PS[:, 4 + m % 2, tt * P:(tt + 1) * P], tiles(1)[:, m % 8, tt * P:(tt + 1) * P],
                                   sub_keysT[:, m, :], start=True, stop=True)
                mm.then_inc(sc_mm, 1)

            for i in range(4):
                for t in weights_block(block_no(PQ, i), tiles(2)):
                    if 4 * i + t:
                        side_scores(4 * i + t - 1)
            side_scores(15)
            pe.wait_ge(sc_done, 16)
            for g in range(16):
                src, tt, half = tiles(2 if g < 8 else 0), (g % 8) // 2, g % 2
                if g >= 2:
                    pe.wait_ge(tok_copy, g - 1)
                for j in range(4):
                    mm = pe.transpose(PS[:, 6 + g % 2, j * P:(j + 1) * P], src[:, 4 * half + j, tt * P:(tt + 1) * P],
                                      ident[:, :])
                mm.then_inc(tok_xpose, 1)
            for g in range(2):
                pe.wait_ge(tok_copy, 15 + g)
                for j in range(4):
                    k = 40 + 4 * g + j
                    mm = pe.matmul(PS[:, 6 + g, j * P:(j + 1) * P], mod[:, k:k + 1].broadcast_to([P, P]), ident[:, :],
                                   start=True, stop=True)
                mm.then_inc(tok_xpose, 1)

            def turn(tt, i, first):
                it = NTURN * tt + i
                for r in range(16):
                    pe.wait_ge(diag_done, 16 * it + r + 1)
                    pe.wait_ge(v_in[r], 16 * it + 16)
                    for half in range(2):
                        mm = pe.matmul(PS[:, 2 * (tt % 2) + half, :], diag[:, r % 4, :], v_ring[r][:, 512 * half:512 * half + 512],
                                       start=False, stop=False, **LAX)
                    mm.then_inc(moe_mm, 1)

            loop = expert_turns(pe, turn)
            for tt in range(TT):
                def clear():
                    pe.wait_ge(fin_a, tt if tt >= 2 else 1)
                    for half in range(2):
                        pe.matmul(PS[:, 2 * (tt % 2) + half, :], zero_row[0:1, 0:P], zero_row[0:1, 0:512],
                                  start=True, stop=False, **LAX)
                loop(tt, before=clear)

        @block.scalar
        def _(act):
            def done(kind, i, t):
                act.wait_ge(tile_done, 4 * block_no(kind, i) + t + 1)

            def rms_squares(a_, src, ready):
                for k in range(KT):
                    if a_ or k >= 2:
                        act.wait_ge(rms_mm, KT * a_ + k - 1 if k >= 2 else KT * a_)
                    ready(k)
                    act.activation(sq[:, k % 2, :], src[:, k, :], ACT.Square).then_inc(rms_sq, 1)
                act.wait_ge(rms_mm, KT * (a_ + 1))
                if a_:
                    act.wait_ge(h_done, KT * a_)
                act.activation(rstd[:, :], PS[:, 4, :], ACT.Sqrt, bias=epsc[:, :]).then_inc(rms_sqrt, 1)

            def head_root(m):
                act.wait_ge(ms_done, m + 1)
                if m >= 2:
                    act.wait_ge(hn_done, m - 1)
                act.activation(rt[:, m % 2, :], PS[:, 4 + m % 2, :], ACT.Sqrt, bias=epsc[:, :]).then_inc(rt_done, 1)

            def head_squares(kind, count, m0, raw):
                for i in range(count):
                    for t in range(4):
                        m = m0 + 4 * i + t
                        done(kind, i, t)
                        if m >= 2:
                            act.wait_ge(ms_done, m - 1)
                        act.activation(sq[:, m % 2, :], PS[:, t, :], ACT.Square).then_inc(sq_done, 1)
                        act.activation(raw[:, 4 * i + t, :], PS[:, t, :], ACT.Copy).then_inc(evac[t], 1)
                        if 4 * i + t:
                            head_root(m - 1)
                head_root(m0 + 4 * count - 1)

            xT = tiles(0)
            for k in range(KT):
                act.wait_ge(xpose, k + 1)
                act.activation(xT[:, k, :], PS[:, 6 + k % 2, :], ACT.Copy).then_inc(xcopy[k % 2], 1)
            act.wait_ge(consts, 7)
            rms_squares(0, xT, lambda k: act.wait_ge(xcopy[k % 2], k // 2 + 1))
            for i in range(2):
                for t in range(4):
                    done(CG, i, t)
                    act.activation(tiles(5)[:, 4 * i + t, :], PS[:, t, :], ACT.Copy).then_inc(evac[t], 1)
            head_squares(Q1, 2, 0, tiles(1))
            head_squares(K1, 2, 8, tiles(3))
            for i in range(2):
                for t in range(4):
                    done(V1, i, t)
                    act.activation(tokens(4)[:, t, 512 * i:512 * i + 512], PS[:, t, :], ACT.Copy).then_inc(evac[t], 1)
            act.wait_ge(par_loaded, 16)
            for t in range(4):
                act.wait_ge(evac[t], evacs(block_no(BG, 1) + 1))
            for kind, dst, c0 in ((GC, 5, 8), (GA, 7, 0)):
                for i in range(2):
                    for t in range(4):
                        done(kind, i, t)
                        act.activation(tiles(dst)[:, 4 * i + t, :], PS[:, t, :], ACT.Sigmoid,
                                       bias=col("b_gate", c0 + 4 * i + t)).then_inc(evac[t], 1)
            prob = tiles(2)

            def exps(i):
                act.wait_ge(s_max, i + 1)
                if i >= 4:
                    act.wait_ge(s_rinv, i - 3)
                w = (i % TT + 1) * P
                act.activation(prob[:, i % 3, 0:w], prob[:, i % 3, 0:w], ACT.Exp, bias=negmax[:, i % 4:i % 4 + 1],
                               accum_out=rowsum[:, i % 4:i % 4 + 1]).then_inc(s_exp, 1)

            def prob_copy(i):
                hd, qt = divmod(i, TT)
                act.wait_ge(p_xpose, i + 1)
                if hd:
                    act.wait_ge(pv_mm, hd)
                act.activation(prob[:, 3:3 + qt + 1, qt * P:(qt + 1) * P],
                               PS[:, 6 + i % 2, 0:(qt + 1) * P].rearrange("p (k q) -> p k q", q=P),
                               ACT.Copy).then_inc(p_copy, 1)

            exps(0)
            for i in range(NH1 * TT):
                if i + 1 < NH1 * TT:
                    exps(i + 1)
                prob_copy(i)
            if stop == 1:
                return
            ev = evacs(block_no(WO, 0) + 1)
            rms_squares(1, xT, lambda k: act.wait_ge(evac[k % 4], ev + k // 4))
            u = tiles(3, 4)
            for i in range(8):
                for t in range(4):
                    done(UP, i, t)
                    act.activation(u[:, 4 * i + t, :], PS[:, t, :], ACT.Relu).then_inc(evac[t], 1)
                    act.wait_ge(evac[t], evacs(block_no(UP, i) + 1))
                    act.activation(u[:, 4 * i + t, :], u[:, 4 * i + t, :], ACT.Square).then_inc(relu_sq, 1)
            if stop == 2:
                return
            act.activation(silu_c[:, :], par[:, COLS["c"]:COLS["c"] + KT], ACT.Silu).then_inc(silu_done, 1)
            ev = evacs(block_no(DN, 3) + 1)
            rms_squares(2, xT, lambda k: act.wait_ge(evac[k % 4], ev + k // 4))
            head_squares(Q2, 1, 16, tiles(1)[:, 0:4, :])
            head_squares(K2, 1, 20, tiles(1)[:, 4:8, :])
            for kind, dst in ((V2, v_sb), (VM, v_ml)):
                for t in range(4):
                    done(kind, 0, t)
                    act.activation(dst[:, t, :], PS[:, t, :], ACT.Copy).then_inc(evac[t], 1)
            for i in range(2):
                for t in range(4):
                    done(QKM, i, t)
                    act.activation(tiles(4)[:, 4 * i + t, :], PS[:, t, :], ACT.Copy).then_inc(evac[t], 1)
            for t in range(4):
                done(OM, 0, t)
                act.activation(tiles(6)[:, t, :], PS[:, t, :], ACT.Sigmoid).then_inc(evac[t], 1)
            for j in range(8):
                act.wait_ge(conv2, 4 * j + 4)
                act.activation(tiles(5)[:, j, :], tmp[:, j % 2, :], ACT.Silu).then_inc(silu_qk, 1)
            act.wait_ge(consts2, 7)
            act.wait_ge(gate_row, 2)
            act.activation(row_a, row_f, ACT.Abs).then_inc(gate_act, 1)
            act.wait_ge(gate_act, 1)
            act.activation(row_a, row_a, ACT.Exp, scale=-1.0).then_inc(gate_act, 1)
            act.wait_ge(gate_act, 2)
            act.activation(row_a, row_a, ACT.Ln, bias=ones_1[0:NML, 0:1]).then_inc(gate_act, 1)

            def soft(c):
                ab = abuf[c % 2]
                act.wait_ge(z_in, c + 1)
                if c >= 2:
                    act.wait_ge(y_mm, c - 1)
                act.activation(ab, zbuf[c % 2], ACT.Abs).then_inc(sb_ln, 1)
                act.wait_ge(sb_ln, 3 * c + 1)
                act.activation(ab, ab, ACT.Exp, scale=-1.0).then_inc(sb_ln, 1)
                act.wait_ge(sb_ln, 3 * c + 2)
                act.activation(ab, ab, ACT.Ln, bias=ones_1[:, 0:1]).then_inc(sb_ln, 1)

            soft(0)
            for c in range(NH2):
                if c + 1 < NH2:
                    soft(c + 1)
                act.wait_ge(sb_arg, c + 1)
                act.activation(abuf[c % 2], zbuf[c % 2], ACT.Exp).then_inc(sb_exp, 1)
            for e in range(NML):
                act.wait_ge(ml_bc, e + 1)
                act.activation(sq[:, e % 2, :], PS[:, 4, :], ACT.Exp, scale=-1.0).then_inc(ml_em, 1)
                act.wait_ge(ml_arg, TT * (e + 1))
                act.activation(zbuf[e % 2], zbuf[e % 2], ACT.Exp).then_inc(ml_exp, 1)
                act.wait_ge(ml_mm, e + 1)
                act.activation(rt[:, e % 2, :], PS[:, 7, :], ACT.Abs).then_inc(ml_abs, 1)
            act.wait_ge(ml_y, NML)
            for m in range(24, 32):
                if m >= 26:
                    act.wait_ge(ms_done, m - 1)
                act.activation(sq[:, m % 2, :], tiles(7)[:, m - 24, :], ACT.Square).then_inc(sq_done, 1)
                if m > 24:
                    head_root(m - 1)
            head_root(31)
            if stop == 3:
                return
            for g in range(4):
                act.wait_ge(sub_xpose, g + 1)
                act.activation(sub_keysT[:, 4 * g:4 * g + 4, :], PS[:, 6 + g % 2, :].rearrange("p (j n) -> p j n", n=NK),
                               ACT.Copy).then_inc(sub_copy, 1)
            ev = evacs(block_no(WO2, 0) + 1)
            rms_squares(3, xT, lambda k: act.wait_ge(evac[k % 4], ev + k // 4))

            def score_copy(m):
                act.wait_ge(sc_mm, m + 1)
                act.activation(scores_sb.rearrange("p (t m) n -> p t m n", m=16)[:, :, m, :],
                               PS[:, 4 + m % 2, :].rearrange("p (t n) -> p t n", n=NK), ACT.Copy).then_inc(sc_done, 1)

            for m in range(16):
                done(PQ, m // 4, m % 4)
                if m >= 8:
                    act.wait_ge(sc_mm, m - 7)
                act.activation(tiles(1)[:, m % 8, :], PS[:, m % 4, :], ACT.Copy).then_inc(evac[m % 4], 1)
                if m:
                    score_copy(m - 1)
            score_copy(15)
            for g in range(18):
                act.wait_ge(tok_xpose, g + 1)
                if g < 16:
                    dst = (h2_tok if g < 8 else x_tok)[:, (g % 8) // 2, 512 * (g % 2):512 * (g % 2) + 512]
                else:
                    dst = gate2[:, 512 * (g - 16):512 * (g - 16) + 512]
                act.activation(dst, PS[:, 6 + g % 2, :], ACT.Copy).then_inc(tok_copy, 1)

            def gate_exps(tt):
                act.wait_ge(gate_arg, tt + 1)
                act.activation(gates[:, tt, :], gates[:, tt, :], ACT.Exp).then_inc(gate_exp, 1)

            def turn(tt, i, first):
                it = NTURN * tt + i

                def gelu(q):
                    act.wait_ge(dot_done, 16 * it + 4 * q + 4)
                    act.activation(acts[:, 4 * q:4 * q + 4], dots[:, 4 * q:4 * q + 4], ACT.Gelu).then_inc(gelu_done, 1)

                def diagonals(q):
                    act.wait_ge(coef_done, 4 * it + q + 1)
                    for j in range(4):
                        r = 4 * q + j
                        if not first or r >= 4:
                            act.wait_ge(moe_mm, 16 * it + r - 3)
                        act.activation(diag[:, j, :], ident[:, :], ACT.Copy, scale=coef[:, r:r + 1]).then_inc(diag_done, 1)

                gelu(0)
                for q in range(1, 4):
                    gelu(q)
                    diagonals(q - 1)
                diagonals(3)

            loop = expert_turns(act, turn)
            gate_exps(0)
            for tt in range(TT):
                if tt + 1 < TT:
                    gate_exps(tt + 1)
                loop(tt)

        @block.vector
        def _(dve):
            def done(kind, i, t):
                dve.wait_ge(tile_done, 4 * block_no(kind, i) + t + 1)

            def rms_scale(a_, src, dst, gain):
                dve.wait_ge(rms_sqrt, a_ + 1)
                dve.reciprocal(rstd[:, :], rstd[:, :]).then_inc(rms_rec, 1)
                dve.wait_ge(rms_rec, a_ + 1)
                for k in range(KT):
                    dve.scalar_tensor_tensor(dst[:, k, :], src[:, k, :], gain(k), rstd[:, :], ALU.mult, ALU.mult)\
                        .then_inc(h_done, 1)

            def head_scale(m, tile, gain):
                dve.wait_ge(rt_done, m + 1)
                dve.reciprocal(rt[:, m % 2, :], rt[:, m % 2, :]).then_inc(rr_done, 1)
                dve.wait_ge(rr_done, m + 1)
                dve.scalar_tensor_tensor(tile, tile, gain, rt[:, m % 2, :], ALU.mult, ALU.mult).then_inc(hn_done, 1)

            xT, u = tiles(0), tiles(5)
            dve.wait_ge(par_loaded, 16)
            rms_scale(0, xT, tiles(2), lambda k: col("norm1", k))
            for i in range(2):
                for t in range(4):
                    done(XC, i, t)
                    dve.wait_ge(evac[t], evacs(block_no(XC, i)))
                    dve.tensor_tensor(u[:, 4 * i + t, :], PS[:, t, :], u[:, 4 * i + t, :], ALU.mult).then_inc(evac[t], 1)
            for i in range(2):
                for t in range(4):
                    j = 4 * i + t
                    c = tmp[:, j % 2, :]
                    dve.wait_ge(evac[t], evacs(block_no(XC, i) + 1))
                    if j >= 2:
                        dve.wait_ge(evac[(j - 2) % 4], evacs(block_no(BG, (j - 2) // 4) + 1))
                    dve.tensor_scalar(c, u[:, j, :], col("conv_w", 16 + j), col("conv_b", j), ALU.mult, ALU.add)\
                        .then_inc(conv_a, 1)
                    dve.wait_ge(conv_a, 2 * j + 1)
                    dve.scalar_tensor_tensor(c[:, 1:S], u[:, j, 0:S - 1], col("conv_w", 8 + j), c[:, 1:S],
                                             ALU.mult, ALU.add).then_inc(conv_a, 1)
                    dve.wait_ge(conv_a, 2 * j + 2)
                    dve.scalar_tensor_tensor(c[:, 2:S], u[:, j, 0:S - 2], col("conv_w", j), c[:, 2:S],
                                             ALU.mult, ALU.add).then_inc(conv_b, 1)
                    dve.wait_ge(conv_b, j + 1)
                    done(BG, i, t)
                    dve.tensor_tensor(tiles(6)[:, j, :], PS[:, t, :], c, ALU.mult).then_inc(evac[t], 1)
            for m in range(16):
                head_scale(m, tiles(1 if m < 8 else 3)[:, m % 8, :], col("q_g" if m < 8 else "k_g"))
            gc, merged = tiles(5), tiles(5)
            for i in range(2):
                for t in range(4):
                    done(CP, i, t)
                    dve.wait_ge(evac[t], evacs(block_no(CP, i)))
                    dve.tensor_tensor(merged[:, 4 * i + t, :], PS[:, t, :], gc[:, 4 * i + t, :], ALU.mult).then_inc(evac[t], 1)
            prob = tiles(2)

            def biased(i):
                hd, qt = divmod(i, TT)
                w = (qt + 1) * P
                dve.wait_ge(s_mm, i + 1)
                dve.wait_ge(toep_masked, hd + 1)
                if i >= 3:
                    dve.wait_ge(p_xpose, i - 2)
                dve.scalar_tensor_tensor(prob[:, i % 3, 0:w], PS[:, 4 + i % 2, 0:w], HD1 ** -0.5,
                                         toep[:, hd % 2, w - 1::-1] if w == S else toep[:, hd % 2, w - 1::-1],
                                         ALU.mult, ALU.add).then_inc(s_biased, 1)
                dve.wait_ge(s_biased, i + 1)
                if i >= 4:
                    dve.wait_ge(s_exp, i - 3)
                dve.tensor_reduce(negmax[:, i % 4:i % 4 + 1], prob[:, i % 3, 0:w], AX.X, ALU.max, negate=True)\
                    .then_inc(s_max, 1)

            def normalise(i):
                w = (i % TT + 1) * P
                dve.wait_ge(s_exp, i + 1)
                if i >= 4:
                    dve.wait_ge(s_norm, i - 3)
                dve.reciprocal(rinv[:, i % 4:i % 4 + 1], rowsum[:, i % 4:i % 4 + 1]).then_inc(s_rinv, 1)
                dve.wait_ge(s_rinv, i + 1)
                dve.tensor_scalar(prob[:, i % 3, 0:w], prob[:, i % 3, 0:w], rinv[:, i % 4:i % 4 + 1], None, ALU.mult)\
                    .then_inc(s_norm, 1)

            dve.wait_ge(tile_done, 4 * block_no(CP, 0))
            n_items = NH1 * TT
            biased(0)
            for i in range(n_items):
                if i + 1 < n_items:
                    biased(i + 1)
                normalise(i)
                if i % (2 * TT) == 2 and i > 2 * TT:
                    pair = i // (2 * TT) - 1
                    dve.wait_ge(pv_mm, 2 * pair + 2)
                    dve.tensor_copy(tiles(6)[:, pair, :], PS[:, pair % 2, :]).then_inc(y_done, 1)
            dve.wait_ge(pv_mm, NH1)
            dve.tensor_copy(tiles(6)[:, NH1 // 2 - 1, :], PS[:, (NH1 // 2 - 1) % 2, :]).then_inc(y_done, 1)
            for i in range(2):
                for t in range(4):
                    j = 4 * i + t
                    done(AP_, i, t)
                    if j >= 2:
                        dve.wait_ge(merged_done, j - 1)
                    dve.wait_ge(evac[t], evacs(block_no(AP_, i)))
                    dve.tensor_tensor(tmp[:, j % 2, :], PS[:, t, :], tiles(7)[:, j, :], ALU.mult).then_inc(evac[t], 1)
                    dve.wait_ge(evac[t], evacs(block_no(AP_, i) + 1))
                    dve.tensor_tensor(merged[:, j, :], merged[:, j, :], tmp[:, j % 2, :], ALU.add).then_inc(merged_done, 1)
            for i in range(2):
                for t in range(4):
                    done(WO, i, t)
                    dve.tensor_tensor(xT[:, 4 * i + t, :], PS[:, t, :], xT[:, 4 * i + t, :], ALU.add).then_inc(evac[t], 1)
            if stop == 1:
                return
            rms_scale(1, xT, tiles(2), lambda k: col("norm2", k))
            for i in (3, 7):
                for t in range(4):
                    done(DN, i, t)
                    dve.tensor_tensor(xT[:, 4 * (i // 4) + t, :], PS[:, t, :], xT[:, 4 * (i // 4) + t, :], ALU.add)\
                        .then_inc(evac[t], 1)
            if stop == 2:
                return
            dve.wait_ge(tile_done, 4 * (block_no(ADA, 11) + 1))
            dve.tensor_tensor(mod[:, :], PS[:, 5, 0:48], par[:, COLS["b_ada"]:COLS["b_ada"] + 48], ALU.add).then_inc(mod_done, 1)
            dve.wait_ge(mod_done, 1)
            for g, name in enumerate(("norm1_2", "norm2_2")):
                dve.scalar_tensor_tensor(gs[:, g, :], mod[:, 24 * g + 8:24 * g + 16], 1.0,
                                         par[:, COLS[name]:COLS[name] + 8], ALU.add, ALU.mult).then_inc(gain_done, 1)
            dve.wait_ge(gain_done, 2)

            def rms_modulate(a_, g, src, dst):
                dve.wait_ge(rms_sqrt, a_ + 1)
                dve.reciprocal(rstd[:, :], rstd[:, :]).then_inc(rms_rec, 1)
                dve.wait_ge(rms_rec, a_ + 1)
                for k in range(KT):
                    dve.scalar_tensor_tensor(dst[:, k, :], src[:, k, :], gs[:, g, k:k + 1], rstd[:, :],
                                             ALU.mult, ALU.mult).then_inc(h_pre, 1)
                    dve.wait_ge(h_pre, KT * g + k + 1)
                    dve.tensor_scalar(dst[:, k, :], dst[:, k, :], mod[:, 24 * g + k:24 * g + k + 1], None, ALU.add)\
                        .then_inc(h_done, 1)

            rms_modulate(2, 0, xT, tiles(2))
            for m in range(16, 24):
                head_scale(m, tiles(1)[:, m - 16, :], col("q_g_2" if m < 20 else "k_g_2"))
            for j in range(8):
                i, t = divmod(j, 4)
                c, u = tmp[:, j % 2, :], tiles(4)[:, j, :]
                dve.wait_ge(evac[t], evacs(block_no(QKM, i) + 1))
                if j >= 2:
                    dve.wait_ge(silu_qk, j - 1)
                dve.tensor_scalar(c, u, col("conv_w_2", 24 + j), None, ALU.mult).then_inc(conv2, 1)
                for back in (1, 2, 3):
                    dve.wait_ge(conv2, 4 * j + back)
                    dve.scalar_tensor_tensor(c[:, back:S], u[:, 0:S - back], col("conv_w_2", 8 * (3 - back) + j),
                                             c[:, back:S], ALU.mult, ALU.add).then_inc(conv2, 1)
            dve.wait_ge(consts2, 7)
            for g, row in enumerate((row_b, row_f)):
                dve.wait_ge(gate_mm, g + 1)
                dve.tensor_scalar(row, PS[0:NML, 4 + g, :], par[0:NML, COLS["b_i"] + g:COLS["b_i"] + g + 1], None, ALU.add)\
                    .then_inc(gate_row, 1)
            dve.wait_ge(gate_act, 3)
            dve.wait_ge(gate_row, 2)
            dve.scalar_tensor_tensor(row_f, row_f, 0.0, row_a, ALU.min, ALU.subtract).then_inc(gate_row, 1)
            dve.wait_ge(gate_row, 3)
            dve.tensor_tensor_scan(row_a, row_one, row_f, 0.0, ALU.mult, ALU.add).then_inc(gate_row, 1)
            dve.wait_ge(gate_row, 4)
            dve.tensor_tensor(row_b, row_b, row_a, ALU.subtract).then_inc(gate_row, 1)
            dve.wait_ge(gate_row, 5)
            dve.tensor_tensor_scan(row_c, row_b, row_b, 0.0, ALU.max, ALU.max).then_inc(gate_row, 1)
            dve.wait_ge(gate_row, 6)
            dve.tensor_scalar(row_negc, row_c, -1.0, None, ALU.mult).then_inc(gate_row, 1)
            dve.tensor_tensor(row_m, row_a, row_c, ALU.add).then_inc(gate_row, 1)
            dve.wait_ge(b_xpose, 1)
            dve.tensor_copy(b_cols[:, :, :], PS[:, 4, 0:TT * NML].rearrange("p (t h) -> p t h", h=NML)).then_inc(gate_row, 1)

            dve.wait_ge(consts2, 17)
            R0 = 3 * 512

            def logits_in(c):
                dve.wait_ge(z_mm, c + 1)
                if c >= 2:
                    dve.wait_ge(sb_exp, c - 1)
                dve.scalar_tensor_tensor(zbuf[c % 2], PSF[:, 0:NCAUSAL], HD2 ** -0.5, neg_strict, ALU.mult, ALU.add)\
                    .then_inc(z_in, 1)

            logits_in(0)
            for c in range(NH2):
                zb, ab = zbuf[c % 2], abuf[c % 2]
                if c + 1 < NH2:
                    logits_in(c + 1)
                dve.wait_ge(sb_ln, 3 * c + 3)
                dve.scalar_tensor_tensor(ab, zb, 0.0, ab, ALU.max, ALU.add).then_inc(sb_sp, 1)
                dve.wait_ge(r_mm, c + 1)
                dve.tensor_tensor(zb, zb, PSF[:, R0:R0 + NCAUSAL], ALU.subtract).then_inc(sb_arg, 1)
                if c % 2 == 0 and c:
                    dve.wait_ge(y_mm, c)
                    dve.tensor_copy(tiles(7)[:, c // 2 - 1, :], PS[:, 6 + (c // 2 - 1) % 2, :]).then_inc(y2_copy, 1)
            dve.wait_ge(y_mm, NH2)
            dve.tensor_copy(tiles(7)[:, NH2 // 2 - 1, :], PS[:, 6 + (NH2 // 2 - 1) % 2, :]).then_inc(y2_copy, 1)
            for e in range(NML):
                zb, ab = zbuf[e % 2], abuf[e % 2]
                dve.wait_ge(ml_bc, e + 1)
                for kt in range(TT):
                    dve.scalar_tensor_tensor(zb[:, causal(kt)], PS[:, 3, kt * P:S], b_cols[:, kt, e:e + 1],
                                             neg_after[:, causal(kt)], ALU.add, ALU.add).then_inc(ml_arg, 1)
                dve.wait_ge(ml_exp, e + 1)
                dve.wait_ge(ml_qk, e + 1)
                dve.scalar_tensor_tensor(ab, PSF[:, 0:NCAUSAL], HDML ** -0.5, zb, ALU.mult, ALU.mult).then_inc(ml_p, 1)
                dve.wait_ge(ml_abs, e + 1)
                dve.tensor_tensor(rt[:, e % 2, :], rt[:, e % 2, :], sq[:, e % 2, :], ALU.max).then_inc(ml_max, 1)
                dve.wait_ge(ml_max, e + 1)
                dve.reciprocal(rt[:, e % 2, :], rt[:, e % 2, :]).then_inc(ml_rec, 1)
                dve.wait_ge(ml_rec, e + 1)
                dve.tensor_tensor(tiles(7)[:, 4 + e, :], PS[:, 6, :], rt[:, e % 2, :], ALU.mult).then_inc(ml_y, 1)
            dve.wait_ge(ml_y, NML)
            for m in range(24, 32):
                head_scale(m, tiles(7)[:, m - 24, :], col("g_out_sb", m - 24))
                if m >= 28:
                    dve.wait_ge(hn_done, m + 1)
                    dve.tensor_tensor(tiles(7)[:, m - 24, :], tiles(7)[:, m - 24, :], tiles(6)[:, m - 28, :], ALU.mult)\
                        .then_inc(mixed_gain, 1)
            for i in range(2):
                for t in range(4):
                    j = 4 * i + t
                    done(WO2, i, t)
                    dve.scalar_tensor_tensor(xT[:, j, :], PS[:, t, :], mod[:, 16 + j:17 + j], xT[:, j, :],
                                             ALU.mult, ALU.add).then_inc(evac[t], 1)
            if stop == 3:
                return
            rms_modulate(3, 1, xT, tiles(2))
            for m in range(16):
                for tt in range(TT):
                    n, at = 16 * tt + m, 5 * (TT * m + tt)
                    sc, v8, i8 = scores_sb[:, n, :], top_v[:, n, :], top_i[:, n, :]
                    dve.wait_ge(sc_done, m + 1)
                    dve.max(v8[:, 0:8], sc).then_inc(top_done, 1)
                    dve.wait_ge(top_done, at + 1)
                    dve.max_index(i8[:, 0:8], v8[:, 0:8], sc).then_inc(top_done, 1)
                    dve.wait_ge(top_done, at + 2)
                    dve.match_replace(sc, v8[:, 0:8], sc, NEG).then_inc(top_done, 1)
                    dve.wait_ge(top_done, at + 3)
                    dve.max(v8[:, 8:16], sc).then_inc(top_done, 1)
                    dve.wait_ge(top_done, at + 4)
                    dve.max_index(i8[:, 8:16], v8[:, 8:16], sc).then_inc(top_done, 1)
            dve.wait_ge(top_done, 5 * 64)
            dve.wait_ge(consts2, 18)
            dve.memset(zero_row[:, :], 0.0).then_inc(fin_a, 1)

            def routing(tt):
                step = [12 * tt]

                def then(ins):
                    ins.then_inc(route, 1)
                    step[0] += 1
                    dve.wait_ge(route, step[0])

                sides_v = top_v[:, 16 * tt:16 * tt + 16, :].rearrange("p (h s) k -> p h s k", s=2)
                sides_f = top_f[:, 16 * tt:16 * tt + 16, :].rearrange("p (h s) k -> p h s k", s=2)
                shape = [P, PH, TOPK, TOPK]
                then(dve.tensor_copy(top_f[:, 16 * tt:16 * tt + 16, :], top_i[:, 16 * tt:16 * tt + 16, :]))
                c4 = cand.rearrange("p (h i j) -> p h i j", i=TOPK, j=TOPK)
                dve.tensor_tensor(c4, sides_v[:, :, 0, :].unsqueeze(3).broadcast_to(shape),
                                  sides_v[:, :, 1, :].unsqueeze(2).broadcast_to(shape), ALU.add).then_inc(cand_done, 1)
                dve.wait_ge(cand_done, tt + 1)
                n = 5 * PH * tt
                for h in range(PH):
                    c, v8, p8 = cand[:, 256 * h:256 * h + 256], best_v[:, 16 * h:16 * h + 16], best_p[:, 16 * h:16 * h + 16]
                    dve.max(v8[:, 0:8], c).then_inc(best_done, 1)
                    dve.wait_ge(best_done, n + 5 * h + 1)
                    dve.max_index(p8[:, 0:8], v8[:, 0:8], c).then_inc(best_done, 1)
                    dve.wait_ge(best_done, n + 5 * h + 2)
                    dve.match_replace(c, v8[:, 0:8], c, NEG).then_inc(best_done, 1)
                    dve.wait_ge(best_done, n + 5 * h + 3)
                    dve.max(v8[:, 8:16], c).then_inc(best_done, 1)
                    dve.wait_ge(best_done, n + 5 * h + 4)
                    dve.max_index(p8[:, 8:16], v8[:, 8:16], c).then_inc(best_done, 1)
                dve.wait_ge(best_done, n + 5 * PH)
                best3 = best_v.rearrange("p (h k) -> p h k", k=TOPK)
                gates3 = gates[:, tt, :].rearrange("p (h k) -> p h k", k=TOPK)
                dve.tensor_tensor(gates3, best3, best3[:, :, 0:1].broadcast_to([P, PH, TOPK]), ALU.subtract)\
                    .then_inc(gate_arg, 1)
                for side in range(2):
                    if side == 0:
                        then(dve.tensor_scalar(pos_u, best_p, 4, None, ALU.logical_shift_right))
                    else:
                        then(dve.tensor_scalar(pos_u, best_p, 15, None, ALU.bitwise_and))
                    then(dve.tensor_copy(pos_f, pos_u))
                    oh = onehot.rearrange("p (s k) -> p s k", k=16)
                    then(dve.tensor_tensor(oh, pos_f.unsqueeze(2).broadcast_to([P, NSLOT, 16]),
                                           iota16[:, :].unsqueeze(1).broadcast_to([P, NSLOT, 16]), ALU.is_equal))
                    oh4 = onehot.rearrange("p (h k i) -> p h k i", k=TOPK, i=16)
                    dve.tensor_tensor(oh4, oh4, sides_f[:, :, side, :].unsqueeze(2).broadcast_to(shape), ALU.mult)\
                        .then_inc(picked, 1)
                    dve.wait_ge(picked, 2 * tt + side + 1)
                    then(dve.tensor_reduce(side_f[side], oh, AX.X, ALU.add))
                dve.wait_ge(gate_exp, tt + 1)
                then(dve.tensor_reduce(smax[:, :], gates3, AX.X, ALU.add))
                then(dve.reciprocal(smax[:, :], smax[:, :]))
                dve.tensor_tensor(gates3, gates3, smax[:, :].unsqueeze(2).broadcast_to([P, PH, TOPK]), ALU.mult)\
                    .then_inc(gated, 1)
                dve.wait_ge(gated, tt + 1)
                then(dve.scalar_tensor_tensor(experts[:, tt, :], side_f[0], float(NK), side_f[1], ALU.mult, ALU.add))

            def turn(tt, i, first):
                it = NTURN * tt + i

                def dot(r):
                    dve.wait_ge(u_in[r % 8], 32 * it + 16 * (r // 8) + 16)
                    if not first or r >= 4:
                        dve.wait_ge(dot_done, 16 * it + r - 3)
                    dve.tensor_tensor_reduce(out=product[r % 4], in0=u_ring[r % 8], in1=h2_tok[:, tt, :], scale=1.0,
                                             scalar=0.0, op0=ALU.mult, op1=ALU.add, accum_out=dots[:, r:r + 1])\
                        .then_inc(dot_done, 1)

                def coefficients(q):
                    dve.wait_ge(gelu_done, 4 * it + q + 1)
                    if not first:
                        dve.wait_ge(diag_done, 16 * it + 4 * q - 12)
                    dve.tensor_tensor(coef[:, 4 * q:4 * q + 4], acts[:, 4 * q:4 * q + 4],
                                      gates[:, tt, bass.ds(16 * i + 4 * q, 4)], ALU.mult).then_inc(coef_done, 1)

                for q in range(4):
                    for j in range(4):
                        dot(4 * q + j)
                    if q:
                        coefficients(q - 1)
                coefficients(3)

            loop = expert_turns(dve, turn)
            dve.wait_ge(tok_copy, 18)
            routing(0)
            for tt in range(TT):
                if tt + 1 < TT:
                    routing(tt + 1)
                loop(tt)
                dve.wait_ge(moe_mm, NSLOT * (tt + 1))
                y = PS[:, 2 * (tt % 2):2 * (tt % 2) + 2, :].rearrange("p b n -> p (b n)")
                dve.wait_ge(dot_done, NSLOT * (tt + 1))
                dve.tensor_tensor(product[0], y, gate2, ALU.mult).then_inc(fin_a, 1)
                dve.wait_ge(fin_a, tt + 2)
                dve.tensor_tensor(x_tok[:, tt, :], x_tok[:, tt, :], product[0], ALU.add).then_inc(fin_b, 1)
                dve.wait_ge(fin_b, tt + 1)


INPUTS = ["x", "w_in", "rel_bias", "w_attn_proj", "w_conv_proj", "w_gate", "w_out", "w_up", "w_down", "w_ada_2",
          "w_in_2", "w_out_2", "w_q_peer_2", "sub_keys_2", "expert_u_2", "expert_v_2"]


def kernel(**inputs):
    import numpy as np
    import concourse.bacc as bacc
    from concourse.bass_utils import run_bass_kernel_spmd as run
    STOP = globals().get("STOP", 99)

    nc = bacc.Bacc("TRN2", target_bir_lowering=False, num_devices=1)
    arrays = {}
    for name in INPUTS:
        v = np.asarray(inputs[name])
        if name.endswith("_2"):
            v = v[0]
        arrays[name] = np.ascontiguousarray(v)
    def columns(v):
        return np.asarray(v).reshape(-1, 128).T

    def pad4(v):
        return np.concatenate([np.asarray(v).reshape(4, 1), np.zeros((124, 1), np.float32)])

    def twice(v):
        return np.tile(np.asarray(v).reshape(64, 1), (2, 1))

    parts = {"norm1": columns(inputs["norm1_g"]), "conv_w": columns(inputs["conv_w"]),
             "conv_b": columns(inputs["conv_b"]), "b_gate": columns(inputs["b_gate"]),
             "norm2": columns(inputs["norm2_g"]), "c": columns(inputs["c_2"]), "b_ada": columns(inputs["b_ada_2"]),
             "norm1_2": columns(inputs["g_norm1_2"]), "norm2_2": columns(inputs["g_norm2_2"]),
             "conv_w_2": columns(inputs["conv_w_2"]), "g_out_sb": columns(inputs["g_out_sb_2"]),
             "g_out_ml": columns(inputs["g_out_ml_2"]), "q_g": twice(inputs["q_norm_g"]),
             "k_g": twice(inputs["k_norm_g"]), "q_g_2": twice(inputs["g_q_sb_2"]), "k_g_2": twice(inputs["g_k_sb_2"]),
             "b_i": pad4(inputs["b_igate_2"]), "b_f": pad4(inputs["b_fgate_2"])}
    arrays["params"] = np.ascontiguousarray(np.concatenate([parts[name] for name in COLS], axis=1))
    arrays = {f"in_{k}": v for k, v in arrays.items()}
    aps = {k[3:]: nc.dram_tensor(k, v.shape, F32, kind="ExternalInput").ap() for k, v in arrays.items()}
    shape = (1, S, D) if STOP > 3 else (128, 8, 512)
    out = nc.dram_tensor("out", shape, F32, kind="ExternalOutput").ap()
    build(nc, aps, out, STOP)
    r = run(nc, [arrays], core_ids=[0])
    return r.results[0]["out"]
```

```python
from contextlib import ExitStack

import concourse.bass as bass
from concourse import mybir

F32 = mybir.dt.float32
U32 = mybir.dt.uint32
ACT = mybir.ActivationFunctionType
ALU = mybir.AluOpType
AX = mybir.AxisListType

S, D, P = 512, 1024, 128
KT, TT = D // P, S // P
EPS = 1e-6
NEG = -1e30
NH1, HD1 = 16, 64
MAX_REL = 256
FF = 4096
NH2, HD2 = 8, 64
NML, HDML = 4, 128
SBW = NH2 * HD2
PH, NK, TOPK = 8, 128, 16
NSLOT = PH * TOPK
NRING = 3

COLS = {}
_at = 0
for _name, _n in [("norm1", 8), ("conv_w", 24), ("conv_b", 8), ("b_gate", 16), ("norm2", 8), ("c", 8),
                  ("b_ada", 48), ("norm1_2", 8), ("norm2_2", 8), ("conv_w_2", 32), ("g_out_sb", 4),
                  ("g_out_ml", 4), ("q_g", 1), ("k_g", 1), ("q_g_2", 1), ("k_g_2", 1), ("b_i", 1), ("b_f", 1)]:
    COLS[_name] = _at
    _at += _n
NCOLS = _at

(CG, XC, BG, Q1, K1, V1, GA, GC, CP, AP_, WO, UP, DN, ADA, Q2, K2, V2, VM, QKM, OM, WO2, PQ) = range(22)
BLOCKS = ([(CG, i) for i in range(2)] + [(XC, i) for i in range(2)] + [(BG, i) for i in range(2)]
          + [(Q1, i) for i in range(2)] + [(K1, i) for i in range(2)] + [(V1, i) for i in range(2)]
          + [(GC, i) for i in range(2)] + [(GA, i) for i in range(2)] + [(CP, i) for i in range(2)]
          + [(AP_, i) for i in range(2)] + [(WO, i) for i in range(2)]
          + [b for i in range(8) for b in ((UP, i), (ADA, i))]
          + [b for i in range(4) for b in ((DN, i), (ADA, 8 + i))] + [(DN, i) for i in range(4, 8)] + [(Q2, 0), (K2, 0), (V2, 0), (VM, 0)]
          + [(QKM, 0), (QKM, 1), (OM, 0), (WO2, 0), (WO2, 1)] + [(PQ, i) for i in range(4)])
NBLOCKS = len(BLOCKS)


def block_no(kind, i=0):
    return BLOCKS.index((kind, i))


def evacuates(n):
    kind, i = BLOCKS[n]
    return kind != ADA and not (kind == DN and i % 4 != 3)


def evacs(n):
    return sum(evacuates(m) for m in range(n))


CAUSAL_AT = {0: 0, 1: 512, 3: 896, 2: 1024}
NCAUSAL = 1280
SCORE_BANK = (4, 5, 2, 3)
LAX = {"skip_group_check": True}


def build(nc, a, out):
    ctx = ExitStack()
    with ctx:
        def sb(name, shape, dt=F32):
            return ctx.enter_context(nc.sbuf_tensor(name, shape, dt))

        def sem(name):
            return ctx.enter_context(nc.semaphore(name))

        slots = sb("slots", [P, 8, 4096])

        def tiles(s, n=1):
            return slots[:, s:s + n, :].rearrange("p s (k t) -> p (s k) t", t=S)

        def tokens(s, width=D):
            return slots[:, s, :].rearrange("p (t d) -> p t d", d=width)

        ring = sb("ring", [P, NRING, KT, 512])
        par = sb("par", [P, NCOLS])
        ident = sb("ident", [P, P])
        ones_d = sb("ones_d", [P, P])
        ones_h = sb("ones_h", [P, P])
        sq = sb("sq", [P, 2, S])
        rt = sb("rt", [P, 2, S])
        rstd = sb("rstd", [P, S])
        tmp = sb("tmp", [P, 2, S])
        toep = sb("toep", [P, 2, S])
        relrow = sb("relrow", [NH1, 640])
        negmax = sb("negmax", [P, 4])
        rowsum = sb("rowsum", [P, 4])
        rinv = sb("rinv", [P, 4])
        epsc = sb("epsc", [P, 1])

        tri = sb("tri", [P, P])
        ones_1 = sb("ones_1", [P, P])
        ones_m = sb("ones_m", [P, P])
        sel = sb("sel", [NML, NML, P])
        w_if = sb("w_if", [P, KT, 2 * NML])
        mod = sb("mod", [P, 48])
        gs = sb("gs", [P, 2, KT])
        silu_c = sb("silu_c", [P, KT])
        b_cols = sb("b_cols", [P, TT, NML])

        experts = sb("experts", [P, TT * NSLOT], U32)
        idx_stage = sb("idx_stage", [P, 16], U32)
        iota16 = sb("iota16", [P, 16])
        dots = sb("dots", [P, 16])
        acts = sb("acts", [P, 16])
        coef = sb("coef", [P, 16])
        soft_sum = sb("soft_sum", [P, 2])
        zero_row = relrow[0:1, 0:S]

        PS = ctx.enter_context(nc.psum_tensor("PS", [P, 8, 512], F32))
        rel_dram = nc.dram_tensor("rel_rows", [NH1, 640], F32, kind="Internal").ap()

        w_loaded = [sem(f"w_loaded{r}") for r in range(NRING)]
        tile_done = sem("tile_done")
        evac = [sem(f"evac{t}") for t in range(4)]
        x_loaded = sem("x_loaded")
        par_loaded = sem("par_loaded")
        consts = sem("consts")
        xpose = sem("xpose")
        xcopy = [sem("xcopy0"), sem("xcopy1")]
        rms_sq, rms_mm, rms_sqrt, rms_rec, h_done = (sem(n) for n in (
            "rms_sq", "rms_mm", "rms_sqrt", "rms_rec", "h_done"))
        sq_done, ms_done, rt_done, rr_done, hn_done = (sem(n) for n in (
            "sq_done", "ms_done", "rt_done", "rr_done", "hn_done"))
        conv_a, conv_b = sem("conv_a"), sem("conv_b")
        u_done = sem("u_done")
        rel_loaded, rel_pad, rel_stored = sem("rel_loaded"), sem("rel_pad"), sem("rel_stored")
        toep_loaded = [sem("toep_loaded0"), sem("toep_loaded1")]
        toep_masked = sem("toep_masked")
        s_mm, s_biased, s_max, s_exp, s_rinv, s_norm, p_xpose, p_copy, pv_mm, y_done = (sem(n) for n in (
            "s_mm", "s_biased", "s_max", "s_exp", "s_rinv", "s_norm", "p_xpose", "p_copy", "pv_mm", "y_done"))
        relu_sq = sem("relu_sq")
        merge_a = sem("merge_a")
        merged_done = sem("merged_done")
        stored = sem("stored")
        ada_acc = sem("ada_acc")
        silu_done, mod_done, gain_done, h_pre = sem("silu_done"), sem("mod_done"), sem("gain_done"), sem("h_pre")
        conv2, silu_qk = sem("conv2"), sem("silu_qk")
        w_if_loaded, gate_mm, gate_act, gate_row, b_xpose = (sem(n) for n in (
            "w_if_loaded", "gate_mm", "gate_act", "gate_row", "b_xpose"))
        consts2 = sem("consts2")
        z_mm, z_in, sb_ln, sb_sp, r_mm, sb_arg, sb_exp, y_mm, y2_copy = (sem(n) for n in (
            "z_mm", "z_in", "sb_ln", "sb_sp", "r_mm", "sb_arg", "sb_exp", "y_mm", "y2_copy"))
        ml_qk, ml_bc, ml_arg, ml_exp, ml_em, ml_p, ml_mm, ml_abs, ml_max, ml_rec, ml_y = (sem(n) for n in (
            "ml_qk", "ml_bc", "ml_arg", "ml_exp", "ml_em", "ml_p", "ml_mm", "ml_abs", "ml_max", "ml_rec", "ml_y"))
        mixed_gain = sem("mixed_gain")
        sub_loaded, sub_xpose, sub_copy, sc_mm, sc_done, top_done, tok_xpose, tok_copy = (sem(n) for n in (
            "sub_loaded", "sub_xpose", "sub_copy", "sc_mm", "sc_done", "top_done", "tok_xpose", "tok_copy"))
        cand_done, best_done, gate_arg, gate_exp, gate_inv, gated, picked, routed, held = (sem(n) for n in (
            "cand_done", "best_done", "gate_arg", "gate_exp", "gate_inv", "gated", "picked", "routed", "held"))
        idx_staged, dot_done, gelu_done, coef_done, diag_done, moe_mm, fin_a, fin_b = (sem(n) for n in (
            "idx_staged", "dot_done", "gelu_done", "coef_done", "diag_done", "moe_mm", "fin_a", "fin_b"))
        paced = sem("paced")
        u_in = [sem(f"u_in{r}") for r in range(8)]
        v_in = [sem(f"v_in{r}") for r in range(16)]

        sub_keys = slots[:, 6, 0:2048].rearrange("p (h c) -> p h c", c=P)
        sub_keysT = slots[:, 6, 2048:4096].rearrange("p (h n) -> p h n", n=NK)
        scores_sb = slots[:, 4:6, :].rearrange("p s (a n) -> p (s a) n", n=NK)
        top_v = slots[:, 3, 0:1024].rearrange("p (m k) -> p m k", k=TOPK)
        top_i = slots[:, 3, 1024:2048].bitcast(U32).rearrange("p (m k) -> p m k", k=TOPK)
        best_v = slots[:, 3, 2048:2064]
        best_p = slots[:, 3, 2064:2080].bitcast(U32)
        pos = slots[:, 3, 2080:2112].bitcast(U32).rearrange("p (s k) -> p s k", k=TOPK)
        picks = slots[:, 3, 2112:2144].rearrange("p (s k) -> p s k", k=TOPK)
        soft_e = slots[:, 3, 2144:2160]
        cand = slots[:, 7, 0:256]
        onehot = slots[:, 7, 256:768]
        gates = toep[:, 0, :]
        diag = toep[:, 1, :].rearrange("p (r q) -> p r q", q=P)
        h2_tok, x_tok = tokens(1), tokens(6)
        gate2 = tmp[:, :, :].rearrange("p a b -> p (a b)")
        u_ring = [slots[:, 4 + r // 4, (r % 4) * D:(r % 4 + 1) * D] for r in range(8)]
        ringf = ring[:, :, :, :].rearrange("p r k n -> p (r k n)")
        v_ring = [ringf[:, r * D:(r + 1) * D] if r < 12 else slots[:, 2, (r - 12) * D:(r - 11) * D] for r in range(16)]
        product = [slots[:, 0, r * D:(r + 1) * D] for r in range(4)]


        NITEM = TT * PH

        def expert_turns(eng, tt, turn, last_apart=False):
            if tt == 0:
                turn(tt, 0, first=True)
            apart = last_apart and tt == TT - 1
            with eng.Fori(1 if tt == 0 else 0, PH - 1 if apart else PH) as i:
                turn(tt, PH * tt + i)
            if apart:
                turn(tt, NITEM - 1, last=True)


        PSF = PS[:, :, :].rearrange("p b n -> p (b n)")
        v_sb = slots[:, 3, 0:2048].rearrange("p (t d) -> p t d", d=SBW)
        v_ml = slots[:, 3, 2048:4096].rearrange("p (t d) -> p t d", d=SBW)
        zbuf = [slots[:, 2, 0:NCAUSAL], slots[:, 2, NCAUSAL:2 * NCAUSAL], slots[:, 6, 2048:2048 + NCAUSAL]]
        abuf = [slots[:, 2, 2 * NCAUSAL:3 * NCAUSAL], slots[:, 4, 0:NCAUSAL], slots[:, 4, 2 * NCAUSAL:3 * NCAUSAL]]
        neg_strict = neg_after = slots[:, 4, NCAUSAL:2 * NCAUSAL]
        row_b, row_f, row_a, row_c = (slots[0:NML, 6, 2048 + 512 * j:2560 + 512 * j] for j in range(4))
        row_one, row_negc, row_m = toep[0:NML, 0, :], toep[0:NML, 1, :], relrow[0:NML, 0:S]

        def causal(kt, base=0):
            return slice(base + CAUSAL_AT[kt], base + CAUSAL_AT[kt] + S - kt * P)

        def col(name, k=0):
            return par[:, COLS[name] + k:COLS[name] + k + 1]

        block = ctx.enter_context(nc.Block())

        def source(n):
            kind, i = BLOCKS[n]
            name, c0 = {
                CG: ("w_in", 4096), XC: ("w_in", 5120), BG: ("w_in", 3072), Q1: ("w_in", 0), K1: ("w_in", 1024),
                V1: ("w_in", 2048), GA: ("w_gate", 0), GC: ("w_gate", 1024), CP: ("w_conv_proj", 0),
                AP_: ("w_attn_proj", 0), WO: ("w_out", 0), UP: ("w_up", 0), ADA: ("w_ada_2", 0),
                Q2: ("w_in_2", 0), K2: ("w_in_2", 512), V2: ("w_in_2", 1024), QKM: ("w_in_2", 1536),
                VM: ("w_in_2", 2560), OM: ("w_in_2", 3072), WO2: ("w_out_2", 0), PQ: ("w_q_peer_2", 0),
                DN: ("w_down", 0)}[kind]
            w, r0 = a[name], 0
            if kind == DN:
                r0, i = 1024 * (i % 4), i // 4
            return w[r0:r0 + 1024, c0 + 512 * i:c0 + 512 * i + 512].rearrange("(k p) n -> p k n", p=P)

        @block.sync
        def _(sp):
            sp.dma_start(tokens(1), a["x"][0].rearrange("(t p) d -> p t d", p=P)).then_inc(x_loaded, 16)
            sp.dma_start(par[:, :], a["params"]).then_inc(par_loaded, 16)
            sp.dma_start(w_if[:, :, :], a["w_in_2"][:, 3584:3592].rearrange("(k p) n -> p k n", p=P))\
                .then_inc(w_if_loaded, 16)
            for n in range(NBLOCKS):
                if n >= NRING:
                    sp.wait_ge(tile_done, 4 * (n - NRING + 1))
                sp.dma_start(ring[:, n % NRING, :, :], source(n)).then_inc(w_loaded[n % NRING], 16)
            for tt in range(TT):
                sp.wait_ge(fin_b, tt + 1)
                sp.dma_start(out[0, tt * P:(tt + 1) * P, :], x_tok[:, tt, :]).then_inc(stored, 16)
            sp.wait_ge(stored, 16 * TT)

        @block.gpsimd
        def _(gp):
            gp.memset(ident[:, :], 0.0).then_inc(consts, 1)
            gp.memset(ones_d[:, :], 1.0 / D).then_inc(consts, 1)
            gp.memset(ones_h[:, :], 1.0 / HD1).then_inc(consts, 1)
            gp.memset(epsc[:, :], EPS).then_inc(consts, 1)
            gp.wait_ge(consts, 4)
            gp.affine_select(out=ident[:, :], in_=ident[:, :], compare_op=ALU.not_equal, fill=1.0, base=0,
                             pattern=[[-1, P]], channel_multiplier=1).then_inc(consts, 1)
            gp.affine_select(out=ones_h[:, 0:64], in_=ones_h[:, 0:64], compare_op=ALU.is_gt, fill=0.0, base=64,
                             pattern=[[0, 64]], channel_multiplier=-1).then_inc(consts, 1)
            gp.affine_select(out=ones_h[:, 64:128], in_=ones_h[:, 64:128], compare_op=ALU.is_ge, fill=0.0, base=-64,
                             pattern=[[0, 64]], channel_multiplier=1).then_inc(consts, 1)
            gp.dma_start(relrow[:, 0:384], a["rel_bias"][:, 129:513]).then_inc(rel_loaded, 16)
            gp.wait_ge(rel_loaded, 16)
            gp.tensor_copy(relrow[:, 384:640], relrow[:, 383:384].broadcast_to([NH1, 256])).then_inc(rel_pad, 1)
            gp.wait_ge(rel_pad, 1)
            gp.dma_start(rel_dram, relrow[:, :]).then_inc(rel_stored, 16)
            gp.wait_ge(rel_stored, 16)
            for h in range(NH1):
                if h >= 2:
                    gp.wait_ge(s_biased, TT * (h - 1))
                gp.dma_start(toep[:, h % 2, :], bass.AP(rel_dram.tensor, h * 640, [[1, P], [1, S]]))\
                    .then_inc(toep_loaded[h % 2], 16)
                gp.wait_ge(toep_loaded[h % 2], 16 * (h // 2 + 1))
                gp.memset(toep[0:64, h % 2, 0:64], NEG).then_inc(toep_masked, 1)
            gp.memset(tri[:, :], 1.0).then_inc(consts2, 1)
            gp.memset(ones_1[:, :], 1.0).then_inc(consts2, 1)
            gp.memset(ones_m[:, :], 1.0 / HDML).then_inc(consts2, 1)
            gp.memset(sel[:, :, :], 0.0).then_inc(consts2, 1)
            gp.wait_ge(s_biased, NH1 * TT)
            gp.memset(row_one, 1.0).then_inc(consts2, 1)
            gp.wait_ge(consts2, 5)
            gp.affine_select(out=tri[:, :], in_=tri[:, :], compare_op=ALU.is_ge, fill=0.0, base=0,
                             pattern=[[-1, P]], channel_multiplier=1).then_inc(consts2, 1)
            gp.affine_select(out=sel[:, :, :], in_=sel[:, :, :], compare_op=ALU.not_equal, fill=1.0, base=0,
                             pattern=[[-1, NML], [0, P]], channel_multiplier=1).then_inc(consts2, 1)
            gp.wait_ge(silu_qk, 8)
            gp.memset(neg_strict, 0.0).then_inc(consts2, 1)
            gp.wait_ge(consts2, 8)
            for kt in range(TT):
                m = neg_strict[:, CAUSAL_AT[kt]:CAUSAL_AT[kt] + P]
                gp.affine_select(out=m, in_=m, compare_op=ALU.is_gt, fill=NEG, base=0,
                                 pattern=[[1, P]], channel_multiplier=-1).then_inc(consts2, 1)
            gp.wait_ge(z_in, NH2)
            gp.memset(neg_after, 0.0).then_inc(consts2, 1)
            gp.wait_ge(consts2, 13)
            for kt in range(TT):
                m = neg_after[:, CAUSAL_AT[kt]:CAUSAL_AT[kt] + P]
                gp.affine_select(out=m, in_=m, compare_op=ALU.is_ge, fill=NEG, base=0,
                                 pattern=[[1, P]], channel_multiplier=-1).then_inc(consts2, 1)
            gp.iota(iota16[:, :], pattern=[[1, 16]], base=0, channel_multiplier=0,
                    allow_small_or_imprecise_dtypes=True).then_inc(consts2, 1)
            gp.wait_ge(mixed_gain, 4)
            gp.dma_start(sub_keys, a["sub_keys_2"].rearrange("h s n c -> n (h s) c")).then_inc(sub_loaded, 16)
            gp.wait_ge(tok_copy, 18)
            gp.wait_ge(top_done, 5 * 64)
            gp.wait_ge(tile_done, 4 * NBLOCKS)

            def turn(tt, it, first=False):
                for half in range(2):
                    if half == 0:
                        gp.wait_ge(routed, it + 1)
                        gp.sem_inc(paced, 1)
                    if not first:
                        gp.wait_ge(moe_mm, 16 * it + 8 * half - 8)
                        gp.sem_inc(paced, 1)
                    gp.tensor_copy(idx_stage[:, 8 * half:8 * half + 8], experts[:, bass.ds(16 * it + 8 * half, 8)])\
                        .then_inc(idx_staged, 1)
                    gp.wait_ge(idx_staged, 2 * it + half + 1)
                    for r in range(8 * half, 8 * half + 8):
                        at = bass.IndirectOffsetOnAxis(ap=idx_stage[:, r:r + 1], axis=0)
                        if not first or r >= 8:
                            gp.wait_ge(dot_done, 16 * it + r - 7)
                        gp.sem_inc(paced, 1)
                        gp.indirect_dma_start(u_ring[r % 8], None, a["expert_u_2"], at).then_inc(u_in[r % 8], 16)
                        gp.indirect_dma_start(v_ring[r], None, a["expert_v_2"], at).then_inc(v_in[r], 16)

            for tt in range(TT):
                expert_turns(gp, tt, turn)

        @block.tensor
        def _(pe):
            def weights_block(n, moving, token_major=False, first=True, last=True):
                pe.wait_ge(w_loaded[n % NRING], 16 * (n // NRING + 1))
                for t in range(4):
                    if first and evacs(n):
                        pe.wait_ge(evac[t], evacs(n))
                    for k in range(KT):
                        w = ring[:, n % NRING, k, :]
                        if token_major:
                            mm = pe.matmul(PS[:, t, :], moving[:, k, t * P:(t + 1) * P], w,
                                           start=first and k == 0, stop=last and k == KT - 1)
                        else:
                            mm = pe.matmul(PS[:, t, :], w[:, t * P:(t + 1) * P], moving[:, k, :],
                                           start=first and k == 0, stop=last and k == KT - 1)
                    mm.then_inc(tile_done, 1)
                    yield t

            def plain(kind, count, moving, token_major=False):
                for i in range(count):
                    for _ in weights_block(block_no(kind, i), moving, token_major):
                        pass

            def rms(a_):
                for k in range(KT):
                    pe.wait_ge(rms_sq, KT * a_ + k + 1)
                    pe.matmul(PS[:, 4, :], ones_d[:, :], sq[:, k % 2, :], start=k == 0, stop=k == KT - 1)\
                        .then_inc(rms_mm, 1)

            def mean_square(m, ones):
                pe.wait_ge(sq_done, m + 1)
                if m >= 2:
                    pe.wait_ge(rt_done, m - 1)
                pe.matmul(PS[:, 4 + m % 2, :], ones, sq[:, m % 2, :], start=True, stop=True).then_inc(ms_done, 1)

            def normed(kind, count, moving, m):
                for i in range(count):
                    for t in weights_block(block_no(kind, i), moving):
                        if 4 * i + t:
                            mean_square(m + 4 * i + t - 1, ones_h[:, :])
                mean_square(m + 4 * count - 1, ones_h[:, :])

            pe.wait_ge(x_loaded, 16)
            pe.wait_ge(consts, 7)
            for k in range(KT):
                if k >= 2:
                    pe.wait_ge(xcopy[k % 2], k // 2)
                for t in range(TT):
                    mm = pe.transpose(PS[:, 6 + k % 2, t * P:(t + 1) * P], tokens(1)[:, t, k * P:(k + 1) * P], ident[:, :])
                mm.then_inc(xpose, 1)
            rms(0)
            h = tiles(2)
            pe.wait_ge(h_done, KT)
            plain(CG, 2, h)
            plain(XC, 2, h)
            plain(BG, 2, h)
            pe.wait_ge(rms_sqrt, 1)
            normed(Q1, 2, h, 0)
            normed(K1, 2, h, 8)
            plain(V1, 2, h, token_major=True)
            plain(GC, 2, h)
            plain(GA, 2, h)
            for t in range(4):
                pe.wait_ge(evac[t], evacs(block_no(BG, 1) + 1))
            plain(CP, 2, tiles(6))

            q, k_, v, prob = tiles(1), tiles(3), tokens(4), tiles(2)
            pe.wait_ge(hn_done, 16)
            for t in range(4):
                pe.wait_ge(evac[t], evacs(block_no(CP, 1) + 1))

            def scores(i):
                hd, qt = divmod(i, TT)
                o = HD1 * (hd % 2)
                if i >= 4:
                    pe.wait_ge(s_biased, i - 3)
                pe.matmul(PS[:, SCORE_BANK[i % 4], 0:(qt + 1) * P], q[o:o + HD1, hd // 2, qt * P:(qt + 1) * P],
                          k_[o:o + HD1, hd // 2, 0:(qt + 1) * P], start=True, stop=True).then_inc(s_mm, 1)

            def transposes(i):
                qt = i % TT
                pe.wait_ge(s_norm, i + 1)
                if i >= 2:
                    pe.wait_ge(p_copy, i - 1)
                for kt in range(qt + 1):
                    mm = pe.transpose(PS[:, 6 + i % 2, kt * P:(kt + 1) * P], prob[:, i % 4, kt * P:(kt + 1) * P],
                                      ident[:, :])
                mm.then_inc(p_xpose, 1)

            def values(hd):
                o = HD1 * (hd % 2)
                pe.wait_ge(p_copy, TT * (hd + 1))
                if hd >= 4 and hd % 2 == 0:
                    pe.wait_ge(y_done, hd // 2 - 1)
                for kt in range(TT):
                    mm = pe.matmul(PS[o:o + HD1, (hd // 2) % 2, kt * P:S], v[:, kt, hd * HD1:(hd + 1) * HD1],
                                   prob[:, 4 + kt, kt * P:S], start=kt == 0, stop=kt == TT - 1)
                mm.then_inc(pv_mm, 1)

            n_items = NH1 * TT
            for i in range(3):
                scores(i)
            for i in range(n_items):
                if i + 3 < n_items:
                    scores(i + 3)
                transposes(i)
                if i and i % TT == 0:
                    values(i // TT - 1)
            values(NH1 - 1)

            pe.wait_ge(y_done, NH1 // 2)
            plain(AP_, 2, tiles(6))
            pe.wait_ge(merged_done, 8)
            plain(WO, 2, tiles(5))
            rms(1)
            pe.wait_ge(h_done, 2 * KT)
            def modulation(i):
                pe.wait_ge(ada_acc, KT * (i + 1))
                for t in range(4):
                    pe.matmul(PS[:, 5, 4 * i + t:4 * i + t + 1], tmp[:, i % 2, t * P:(t + 1) * P], ones_1[:, 0:1],
                              start=True, stop=True).then_inc(tile_done, 1)

            pe.wait_ge(consts2, 7)
            pe.wait_ge(rt_done, 16)
            for i in range(8):
                for _ in weights_block(block_no(UP, i), tiles(2)):
                    pass
                modulation(i)
            for i in range(8):
                if i < 4:
                    pe.wait_ge(relu_sq, 8 * i + 8)
                for _ in weights_block(block_no(DN, i), tiles(3, 4)[:, 8 * (i % 4):8 * (i % 4) + 8, :],
                                       first=i % 4 == 0, last=i % 4 == 3):
                    pass
                if i < 4:
                    modulation(8 + i)
            rms(2)
            pe.wait_ge(h_done, 3 * KT)
            pe.wait_ge(mod_done, 1)
            h = tiles(2)
            normed(Q2, 1, h, 16)
            normed(K2, 1, h, 20)
            plain(V2, 1, h, token_major=True)
            plain(VM, 1, h, token_major=True)
            plain(QKM, 2, h)
            plain(OM, 1, h)
            pe.wait_ge(w_if_loaded, 16)
            pe.wait_ge(rt_done, 24)
            for g in range(2):
                for k in range(KT):
                    mm = pe.matmul(PS[0:NML, 4 + g, :], w_if[:, k, g * NML:(g + 1) * NML], h[:, k, :],
                                   start=k == 0, stop=k == KT - 1)
                mm.then_inc(gate_mm, 1)
            pe.wait_ge(gate_row, 5)
            for kt in range(TT):
                mm = pe.transpose(PS[:, 4, kt * NML:(kt + 1) * NML], row_b[:, kt * P:(kt + 1) * P], ident[0:NML, 0:NML])
            mm.then_inc(b_xpose, 1)
            pe.wait_ge(gate_row, 9)

            q, k_ = tiles(1)[:, 0:4, :], tiles(1)[:, 4:8, :]
            R0 = 3 * 512
            pe.wait_ge(hn_done, 24)
            pe.wait_ge(consts2, 7)
            for t in range(4):
                pe.wait_ge(evac[t], evacs(block_no(OM) + 1))

            def logits(c):
                o = HD2 * (c % 2)
                if c:
                    pe.wait_ge(z_in, c)
                for kt in range(TT):
                    mm = pe.matmul(PSF[:, causal(kt)], k_[o:o + HD2, c // 2, kt * P:(kt + 1) * P],
                                   q[o:o + HD2, c // 2, kt * P:S], start=kt in (0, 1, 2), stop=True, **LAX)
                mm.then_inc(z_mm, 1)

            def sums(c):
                ab = abuf[c % 3]
                pe.wait_ge(sb_sp, c + 1)
                if c:
                    pe.wait_ge(sb_arg, c)
                for kt in range(TT):
                    out_ = causal(kt, R0)
                    mm = pe.matmul(PSF[:, out_], tri[:, :], ab[:, causal(kt)], start=kt in (0, 1, 2), stop=True, **LAX)
                    for k2 in range(kt + 1, TT):
                        sub = slice(out_.start + (k2 - kt) * P, out_.stop)
                        mm = pe.matmul(PSF[:, sub], ones_1[:, :], ab[:, causal(k2)], start=False, stop=True, **LAX)
                mm.then_inc(r_mm, 1)

            def sb_values(c):
                o = HD2 * (c % 2)
                pe.wait_ge(sb_exp, c + 1)
                if c >= 4 and c % 2 == 0:
                    pe.wait_ge(y2_copy, c // 2 - 1)
                for kt in range(TT):
                    mm = pe.matmul(PS[o:o + HD2, 6 + (c // 2) % 2, kt * P:S], v_sb[:, kt, c * HD2:(c + 1) * HD2],
                                   abuf[c % 3][:, causal(kt)], start=kt == 0, stop=kt == TT - 1)
                mm.then_inc(y_mm, 1)

            logits(0)
            logits(1)
            sums(0)
            for c in range(NH2):
                if c + 2 < NH2:
                    logits(c + 2)
                if c + 1 < NH2:
                    sums(c + 1)
                sb_values(c)

            q, k_ = tiles(5)[:, 0:4, :], tiles(5)[:, 4:8, :]
            pe.wait_ge(y2_copy, NH2 // 2)
            pe.wait_ge(sb_arg, NH2)
            pe.wait_ge(silu_qk, 8)
            def ml_scores(e):
                if e:
                    pe.wait_ge(ml_arg, TT * e)
                    pe.wait_ge(ml_em, e)
                pe.matmul(PS[:, 3, :], sel[:, e, :], row_negc, start=True, stop=True)
                pe.matmul(PS[:, 4, :], sel[:, e, :], row_m, start=True, stop=True).then_inc(ml_bc, 1)
                if e:
                    pe.wait_ge(ml_p, e)
                for kt in range(TT):
                    mm = pe.matmul(PSF[:, causal(kt)], k_[:, e, kt * P:(kt + 1) * P], q[:, e, kt * P:S],
                                   start=kt in (0, 1, 2), stop=True, **LAX)
                mm.then_inc(ml_qk, 1)

            def ml_values(e):
                pe.wait_ge(ml_p, e + 1)
                if e:
                    pe.wait_ge(ml_y, e)
                for kt in range(TT):
                    pr = abuf[e % 2][:, causal(kt)]
                    pe.matmul(PS[:, 6, kt * P:S], v_ml[:, kt, e * HDML:(e + 1) * HDML], pr, start=kt == 0, stop=kt == TT - 1)
                for kt in range(TT):
                    pr = abuf[e % 2][:, causal(kt)]
                    mm = pe.matmul(PS[:, 7, kt * P:S], ones_1[:, :], pr, start=kt == 0, stop=kt == TT - 1)
                mm.then_inc(ml_mm, 1)

            ml_scores(0)
            for e in range(NML):
                if e + 1 < NML:
                    ml_scores(e + 1)
                ml_values(e)
            pe.wait_ge(ml_y, NML)
            for m in range(24, 32):
                mean_square(m, ones_h[:, :] if m < 28 else ones_m[:, :])
            pe.wait_ge(mixed_gain, 4)
            pe.wait_ge(hn_done, 32)
            plain(WO2, 2, tiles(7))
            pe.wait_ge(sub_loaded, 16)
            for g in range(4):
                if g >= 2:
                    pe.wait_ge(sub_copy, g - 1)
                for j in range(4):
                    mm = pe.transpose(PS[:, 6 + g % 2, j * P:(j + 1) * P], sub_keys[:, 4 * g + j, :], ident[:, :])
                mm.then_inc(sub_xpose, 1)
            rms(3)
            pe.wait_ge(h_done, 4 * KT)
            pe.wait_ge(sub_copy, 4)
            pe.wait_ge(rms_sqrt, 4)

            def side_scores(m):
                pe.wait_ge(evac[m % 4], evacs(block_no(PQ, m // 4) + 1))
                if m >= 2:
                    pe.wait_ge(sc_done, m - 1)
                for tt in range(TT):
                    mm = pe.matmul(PS[:, 4 + m % 2, tt * P:(tt + 1) * P], tiles(1)[:, m % 8, tt * P:(tt + 1) * P],
                                   sub_keysT[:, m, :], start=True, stop=True)
                mm.then_inc(sc_mm, 1)

            for i in range(4):
                for t in weights_block(block_no(PQ, i), tiles(2)):
                    if 4 * i + t:
                        side_scores(4 * i + t - 1)
            side_scores(15)
            pe.wait_ge(sc_done, 16)
            for g in range(16):
                src, tt, half = tiles(2 if g < 8 else 0), (g % 8) // 2, g % 2
                if g >= 2:
                    pe.wait_ge(tok_copy, g - 1)
                for j in range(4):
                    mm = pe.transpose(PS[:, 6 + g % 2, j * P:(j + 1) * P], src[:, 4 * half + j, tt * P:(tt + 1) * P],
                                      ident[:, :])
                mm.then_inc(tok_xpose, 1)
            for g in range(2):
                pe.wait_ge(tok_copy, 15 + g)
                for j in range(4):
                    k = 40 + 4 * g + j
                    mm = pe.matmul(PS[:, 6 + g, j * P:(j + 1) * P], mod[:, k:k + 1].broadcast_to([P, P]), ident[:, :],
                                   start=True, stop=True)
                mm.then_inc(tok_xpose, 1)

            def turn(tt, it, first=False):
                for r in range(16):
                    pe.wait_ge(diag_done, 16 * it + r + 1)
                    pe.wait_ge(v_in[r], 16 * it + 16)
                    for half in range(2):
                        mm = pe.matmul(PS[:, 2 * (tt % 2) + half, :], diag[:, r % 4, :], v_ring[r][:, 512 * half:512 * half + 512],
                                       start=False, stop=False, **LAX)
                    mm.then_inc(moe_mm, 1)

            for tt in range(TT):
                pe.wait_ge(fin_a, tt if tt >= 2 else 1)
                for half in range(2):
                    pe.matmul(PS[:, 2 * (tt % 2) + half, :], zero_row[0:1, 0:P], zero_row[0:1, 0:512],
                              start=True, stop=False, **LAX)
                expert_turns(pe, tt, turn)

        @block.scalar
        def _(act):
            def done(kind, i, t):
                act.wait_ge(tile_done, 4 * block_no(kind, i) + t + 1)

            def rms_squares(a_, src, ready):
                for k in range(KT):
                    if a_ or k >= 2:
                        act.wait_ge(rms_mm, KT * a_ + k - 1 if k >= 2 else KT * a_)
                    ready(k)
                    act.activation(sq[:, k % 2, :], src[:, k, :], ACT.Square).then_inc(rms_sq, 1)
                act.wait_ge(rms_mm, KT * (a_ + 1))
                if a_:
                    act.wait_ge(h_done, KT * a_)
                act.activation(rstd[:, :], PS[:, 4, :], ACT.Sqrt, bias=epsc[:, :]).then_inc(rms_sqrt, 1)

            def head_root(m):
                act.wait_ge(ms_done, m + 1)
                if m >= 2:
                    act.wait_ge(hn_done, m - 1)
                act.activation(rt[:, m % 2, :], PS[:, 4 + m % 2, :], ACT.Sqrt, bias=epsc[:, :]).then_inc(rt_done, 1)

            def head_squares(kind, count, m0, raw):
                for i in range(count):
                    for t in range(4):
                        m = m0 + 4 * i + t
                        done(kind, i, t)
                        if m >= 2:
                            act.wait_ge(ms_done, m - 1)
                        act.activation(sq[:, m % 2, :], PS[:, t, :], ACT.Square).then_inc(sq_done, 1)
                        act.activation(raw[:, 4 * i + t, :], PS[:, t, :], ACT.Copy).then_inc(evac[t], 1)
                        if 4 * i + t:
                            head_root(m - 1)
                head_root(m0 + 4 * count - 1)

            xT = tiles(0)
            for k in range(KT):
                act.wait_ge(xpose, k + 1)
                act.activation(xT[:, k, :], PS[:, 6 + k % 2, :], ACT.Copy).then_inc(xcopy[k % 2], 1)
            act.wait_ge(consts, 7)
            rms_squares(0, xT, lambda k: act.wait_ge(xcopy[k % 2], k // 2 + 1))
            for i in range(2):
                for t in range(4):
                    done(CG, i, t)
                    act.activation(tiles(5)[:, 4 * i + t, :], PS[:, t, :], ACT.Copy).then_inc(evac[t], 1)
            head_squares(Q1, 2, 0, tiles(1))
            head_squares(K1, 2, 8, tiles(3))
            for i in range(2):
                for t in range(4):
                    done(V1, i, t)
                    act.activation(tokens(4)[:, t, 512 * i:512 * i + 512], PS[:, t, :], ACT.Copy).then_inc(evac[t], 1)
            act.wait_ge(par_loaded, 16)
            for t in range(4):
                act.wait_ge(evac[t], evacs(block_no(BG, 1) + 1))
            for kind, dst, c0 in ((GC, 5, 8), (GA, 7, 0)):
                for i in range(2):
                    for t in range(4):
                        done(kind, i, t)
                        act.activation(tiles(dst)[:, 4 * i + t, :], PS[:, t, :], ACT.Sigmoid,
                                       bias=col("b_gate", c0 + 4 * i + t)).then_inc(evac[t], 1)
            prob = tiles(2)

            def exps(i):
                act.wait_ge(s_max, i + 1)
                if i >= 4:
                    act.wait_ge(s_rinv, i - 3)
                w = (i % TT + 1) * P
                act.activation(prob[:, i % 4, 0:w], prob[:, i % 4, 0:w], ACT.Exp, bias=negmax[:, i % 4:i % 4 + 1],
                               accum_out=rowsum[:, i % 4:i % 4 + 1]).then_inc(s_exp, 1)

            def normalise(i):
                w = (i % TT + 1) * P
                act.wait_ge(s_rinv, i + 1)
                act.activation(prob[:, i % 4, 0:w], prob[:, i % 4, 0:w], ACT.Copy, scale=rinv[:, i % 4:i % 4 + 1])\
                    .then_inc(s_norm, 1)

            def prob_copy(i):
                hd, qt = divmod(i, TT)
                act.wait_ge(p_xpose, i + 1)
                if hd:
                    act.wait_ge(pv_mm, hd)
                act.activation(prob[:, 4:4 + qt + 1, qt * P:(qt + 1) * P],
                               PS[:, 6 + i % 2, 0:(qt + 1) * P].rearrange("p (k q) -> p k q", q=P),
                               ACT.Copy).then_inc(p_copy, 1)

            exps(0)
            for i in range(NH1 * TT):
                if i + 1 < NH1 * TT:
                    exps(i + 1)
                normalise(i)
                if i:
                    prob_copy(i - 1)
            prob_copy(NH1 * TT - 1)
            act.activation(silu_c[:, :], par[:, COLS["c"]:COLS["c"] + KT], ACT.Silu).then_inc(silu_done, 1)
            ev = evacs(block_no(WO, 0) + 1)
            rms_squares(1, xT, lambda k: act.wait_ge(evac[k % 4], ev + k // 4))
            u = tiles(3, 4)
            for i in range(8):
                for t in range(4):
                    done(UP, i, t)
                    act.activation(u[:, 4 * i + t, :], PS[:, t, :], ACT.Relu).then_inc(evac[t], 1)
                    act.wait_ge(evac[t], evacs(block_no(UP, i) + 1))
                    act.activation(u[:, 4 * i + t, :], u[:, 4 * i + t, :], ACT.Square).then_inc(relu_sq, 1)
            ev = evacs(block_no(DN, 3) + 1)
            rms_squares(2, xT, lambda k: act.wait_ge(evac[k % 4], ev + k // 4))
            head_squares(Q2, 1, 16, tiles(1)[:, 0:4, :])
            head_squares(K2, 1, 20, tiles(1)[:, 4:8, :])
            for kind, dst in ((V2, v_sb), (VM, v_ml)):
                for t in range(4):
                    done(kind, 0, t)
                    act.activation(dst[:, t, :], PS[:, t, :], ACT.Copy).then_inc(evac[t], 1)
            for i in range(2):
                for t in range(4):
                    done(QKM, i, t)
                    act.activation(tiles(4)[:, 4 * i + t, :], PS[:, t, :], ACT.Copy).then_inc(evac[t], 1)
            for t in range(4):
                done(OM, 0, t)
                act.activation(tiles(6)[:, t, :], PS[:, t, :], ACT.Sigmoid).then_inc(evac[t], 1)
            for j in range(8):
                act.wait_ge(conv2, 4 * j + 4)
                act.activation(tiles(5)[:, j, :], tmp[:, j % 2, :], ACT.Silu).then_inc(silu_qk, 1)
            act.wait_ge(consts2, 7)
            act.wait_ge(gate_row, 2)
            act.activation(row_a, row_f, ACT.Abs).then_inc(gate_act, 1)
            act.wait_ge(gate_act, 1)
            act.activation(row_a, row_a, ACT.Exp, scale=-1.0).then_inc(gate_act, 1)
            act.wait_ge(gate_act, 2)
            act.activation(row_a, row_a, ACT.Ln, bias=ones_1[0:NML, 0:1]).then_inc(gate_act, 1)

            def soft(c):
                ab = abuf[c % 3]
                act.wait_ge(z_in, c + 1)
                if c >= 3:
                    act.wait_ge(y_mm, c - 2)
                act.activation(ab, zbuf[c % 3], ACT.Abs).then_inc(sb_ln, 1)
                act.wait_ge(sb_ln, 3 * c + 1)
                act.activation(ab, ab, ACT.Exp, scale=-1.0).then_inc(sb_ln, 1)
                act.wait_ge(sb_ln, 3 * c + 2)
                act.activation(ab, ab, ACT.Ln, bias=ones_1[:, 0:1]).then_inc(sb_ln, 1)

            soft(0)
            soft(1)
            for c in range(NH2):
                act.wait_ge(sb_arg, c + 1)
                act.activation(abuf[c % 3], zbuf[c % 3], ACT.Exp).then_inc(sb_exp, 1)
                if c + 2 < NH2:
                    soft(c + 2)
            def ml_exps(e):
                act.wait_ge(ml_bc, e + 1)
                if e >= 2:
                    act.wait_ge(ml_max, e - 1)
                act.activation(sq[:, e % 2, :], PS[:, 4, :], ACT.Exp, scale=-1.0).then_inc(ml_em, 1)
                act.wait_ge(ml_arg, TT * (e + 1))
                act.activation(zbuf[e % 2], zbuf[e % 2], ACT.Exp).then_inc(ml_exp, 1)

            ml_exps(0)
            for e in range(NML):
                if e + 1 < NML:
                    ml_exps(e + 1)
                act.wait_ge(ml_mm, e + 1)
                if e >= 2:
                    act.wait_ge(ml_y, e - 1)
                act.activation(rt[:, e % 2, :], PS[:, 7, :], ACT.Abs).then_inc(ml_abs, 1)
            act.wait_ge(ml_y, NML)
            for m in range(24, 32):
                if m >= 26:
                    act.wait_ge(ms_done, m - 1)
                act.activation(sq[:, m % 2, :], tiles(7)[:, m - 24, :], ACT.Square).then_inc(sq_done, 1)
                if m > 24:
                    head_root(m - 1)
            head_root(31)
            for g in range(4):
                act.wait_ge(sub_xpose, g + 1)
                act.activation(sub_keysT[:, 4 * g:4 * g + 4, :], PS[:, 6 + g % 2, :].rearrange("p (j n) -> p j n", n=NK),
                               ACT.Copy).then_inc(sub_copy, 1)
            ev = evacs(block_no(WO2, 0) + 1)
            rms_squares(3, xT, lambda k: act.wait_ge(evac[k % 4], ev + k // 4))

            def score_copy(m):
                act.wait_ge(sc_mm, m + 1)
                act.activation(scores_sb.rearrange("p (t m) n -> p t m n", m=16)[:, :, m, :],
                               PS[:, 4 + m % 2, :].rearrange("p (t n) -> p t n", n=NK), ACT.Copy).then_inc(sc_done, 1)

            for m in range(16):
                done(PQ, m // 4, m % 4)
                if m >= 8:
                    act.wait_ge(sc_mm, m - 7)
                act.activation(tiles(1)[:, m % 8, :], PS[:, m % 4, :], ACT.Copy).then_inc(evac[m % 4], 1)
                if m:
                    score_copy(m - 1)
            score_copy(15)
            for g in range(18):
                act.wait_ge(tok_xpose, g + 1)
                if g < 16:
                    dst = (h2_tok if g < 8 else x_tok)[:, (g % 8) // 2, 512 * (g % 2):512 * (g % 2) + 512]
                else:
                    dst = gate2[:, 512 * (g - 16):512 * (g - 16) + 512]
                act.activation(dst, PS[:, 6 + g % 2, :], ACT.Copy).then_inc(tok_copy, 1)

            def gate_exps(item):
                act.wait_ge(gate_arg, item + 1)
                act.activation(soft_e, soft_e, ACT.Exp, accum_out=soft_sum[:, 0:1]).then_inc(gate_exp, 1)

            def turn(tt, it, first=False, last=False):
                if not last:
                    gate_exps(it + 1)

                def gelu(q):
                    act.wait_ge(dot_done, 16 * it + 4 * q + 4)
                    act.activation(acts[:, 4 * q:4 * q + 4], dots[:, 4 * q:4 * q + 4], ACT.Gelu).then_inc(gelu_done, 1)

                def diagonals(q):
                    act.wait_ge(coef_done, 4 * it + q + 1)
                    for j in range(4):
                        r = 4 * q + j
                        if not first or r >= 4:
                            act.wait_ge(moe_mm, 16 * it + r - 3)
                        act.activation(diag[:, j, :], ident[:, :], ACT.Copy, scale=coef[:, r:r + 1]).then_inc(diag_done, 1)

                gelu(0)
                for q in range(1, 4):
                    gelu(q)
                    diagonals(q - 1)
                diagonals(3)

            gate_exps(0)
            for tt in range(TT):
                expert_turns(act, tt, turn, last_apart=True)

        @block.vector
        def _(dve):
            def done(kind, i, t):
                dve.wait_ge(tile_done, 4 * block_no(kind, i) + t + 1)

            def rms_scale(a_, src, dst, gain):
                dve.wait_ge(rms_sqrt, a_ + 1)
                dve.reciprocal(rstd[:, :], rstd[:, :]).then_inc(rms_rec, 1)
                dve.wait_ge(rms_rec, a_ + 1)
                for k in range(KT):
                    dve.scalar_tensor_tensor(dst[:, k, :], src[:, k, :], gain(k), rstd[:, :], ALU.mult, ALU.mult)\
                        .then_inc(h_done, 1)

            def head_scale(m, tile, gain):
                dve.wait_ge(rt_done, m + 1)
                dve.reciprocal(rt[:, m % 2, :], rt[:, m % 2, :]).then_inc(rr_done, 1)
                dve.wait_ge(rr_done, m + 1)
                dve.scalar_tensor_tensor(tile, tile, gain, rt[:, m % 2, :], ALU.mult, ALU.mult).then_inc(hn_done, 1)

            xT, u = tiles(0), tiles(5)
            dve.wait_ge(par_loaded, 16)
            rms_scale(0, xT, tiles(2), lambda k: col("norm1", k))
            for i in range(2):
                for t in range(4):
                    done(XC, i, t)
                    dve.wait_ge(evac[t], evacs(block_no(XC, i)))
                    dve.tensor_tensor(u[:, 4 * i + t, :], PS[:, t, :], u[:, 4 * i + t, :], ALU.mult).then_inc(evac[t], 1)
            for i in range(2):
                for t in range(4):
                    j = 4 * i + t
                    c = tmp[:, j % 2, :]
                    dve.wait_ge(evac[t], evacs(block_no(XC, i) + 1))
                    if j >= 2:
                        dve.wait_ge(evac[(j - 2) % 4], evacs(block_no(BG, (j - 2) // 4) + 1))
                    dve.tensor_scalar(c, u[:, j, :], col("conv_w", 16 + j), col("conv_b", j), ALU.mult, ALU.add)\
                        .then_inc(conv_a, 1)
                    dve.wait_ge(conv_a, 2 * j + 1)
                    dve.scalar_tensor_tensor(c[:, 1:S], u[:, j, 0:S - 1], col("conv_w", 8 + j), c[:, 1:S],
                                             ALU.mult, ALU.add).then_inc(conv_a, 1)
                    dve.wait_ge(conv_a, 2 * j + 2)
                    dve.scalar_tensor_tensor(c[:, 2:S], u[:, j, 0:S - 2], col("conv_w", j), c[:, 2:S],
                                             ALU.mult, ALU.add).then_inc(conv_b, 1)
                    dve.wait_ge(conv_b, j + 1)
                    done(BG, i, t)
                    dve.tensor_tensor(tiles(6)[:, j, :], PS[:, t, :], c, ALU.mult).then_inc(evac[t], 1)
            for m in range(16):
                head_scale(m, tiles(1 if m < 8 else 3)[:, m % 8, :], col("q_g" if m < 8 else "k_g"))
            gc, merged = tiles(5), tiles(5)
            for i in range(2):
                for t in range(4):
                    done(CP, i, t)
                    dve.wait_ge(evac[t], evacs(block_no(CP, i)))
                    dve.tensor_tensor(merged[:, 4 * i + t, :], PS[:, t, :], gc[:, 4 * i + t, :], ALU.mult).then_inc(evac[t], 1)
            prob = tiles(2)

            def biased(i):
                hd, qt = divmod(i, TT)
                w = (qt + 1) * P
                dve.wait_ge(s_mm, i + 1)
                dve.wait_ge(toep_masked, hd + 1)
                if i >= 4:
                    dve.wait_ge(p_xpose, i - 3)
                dve.scalar_tensor_tensor(prob[:, i % 4, 0:w], PS[:, SCORE_BANK[i % 4], 0:w], HD1 ** -0.5,
                                         toep[:, hd % 2, w - 1::-1],
                                         ALU.mult, ALU.add).then_inc(s_biased, 1)
                dve.wait_ge(s_biased, i + 1)
                if i >= 4:
                    dve.wait_ge(s_exp, i - 3)
                dve.tensor_reduce(negmax[:, i % 4:i % 4 + 1], prob[:, i % 4, 0:w], AX.X, ALU.max, negate=True)\
                    .then_inc(s_max, 1)

            def inverse(i):
                dve.wait_ge(s_exp, i + 1)
                if i >= 4:
                    dve.wait_ge(s_norm, i - 3)
                dve.reciprocal(rinv[:, i % 4:i % 4 + 1], rowsum[:, i % 4:i % 4 + 1]).then_inc(s_rinv, 1)

            dve.wait_ge(tile_done, 4 * block_no(CP, 0))
            n_items = NH1 * TT
            biased(0)
            biased(1)
            for i in range(n_items):
                if i + 2 < n_items:
                    biased(i + 2)
                inverse(i)
                if i % (2 * TT) == 2 and i > 2 * TT:
                    pair = i // (2 * TT) - 1
                    dve.wait_ge(pv_mm, 2 * pair + 2)
                    dve.tensor_copy(tiles(6)[:, pair, :], PS[:, pair % 2, :]).then_inc(y_done, 1)
            dve.wait_ge(pv_mm, NH1)
            dve.tensor_copy(tiles(6)[:, NH1 // 2 - 1, :], PS[:, (NH1 // 2 - 1) % 2, :]).then_inc(y_done, 1)
            for i in range(2):
                for t in range(4):
                    j = 4 * i + t
                    done(AP_, i, t)
                    if j >= 2:
                        dve.wait_ge(merged_done, j - 1)
                    dve.wait_ge(evac[t], evacs(block_no(AP_, i)))
                    dve.tensor_tensor(tmp[:, j % 2, :], PS[:, t, :], tiles(7)[:, j, :], ALU.mult).then_inc(evac[t], 1)
                    dve.wait_ge(evac[t], evacs(block_no(AP_, i) + 1))
                    dve.tensor_tensor(merged[:, j, :], merged[:, j, :], tmp[:, j % 2, :], ALU.add).then_inc(merged_done, 1)
            for i in range(2):
                for t in range(4):
                    done(WO, i, t)
                    dve.tensor_tensor(xT[:, 4 * i + t, :], PS[:, t, :], xT[:, 4 * i + t, :], ALU.add).then_inc(evac[t], 1)
            rms_scale(1, xT, tiles(2), lambda k: col("norm2", k))

            def modulation(i):
                n, acc = block_no(ADA, i), tmp[:, i % 2, :]
                dve.wait_ge(w_loaded[n % NRING], 16 * (n // NRING + 1))
                if i >= 2:
                    dve.wait_ge(tile_done, 4 * (block_no(ADA, i - 2) + 1))
                dve.tensor_scalar(acc, ring[:, n % NRING, 0, :], silu_c[:, 0:1], None, ALU.mult).then_inc(ada_acc, 1)
                for k in range(1, KT):
                    dve.wait_ge(ada_acc, KT * i + k)
                    dve.scalar_tensor_tensor(acc, ring[:, n % NRING, k, :], silu_c[:, k:k + 1], acc, ALU.mult, ALU.add)\
                        .then_inc(ada_acc, 1)

            def residual(i):
                for t in range(4):
                    done(DN, i, t)
                    dve.tensor_tensor(xT[:, 4 * (i // 4) + t, :], PS[:, t, :], xT[:, 4 * (i // 4) + t, :], ALU.add)\
                        .then_inc(evac[t], 1)

            dve.wait_ge(silu_done, 1)
            for i in range(11):
                modulation(i)
            residual(3)
            modulation(11)
            residual(7)
            dve.wait_ge(tile_done, 4 * (block_no(ADA, 11) + 1))
            dve.tensor_tensor(mod[:, :], PS[:, 5, 0:48], par[:, COLS["b_ada"]:COLS["b_ada"] + 48], ALU.add).then_inc(mod_done, 1)
            dve.wait_ge(mod_done, 1)
            for g, name in enumerate(("norm1_2", "norm2_2")):
                dve.scalar_tensor_tensor(gs[:, g, :], mod[:, 24 * g + 8:24 * g + 16], 1.0,
                                         par[:, COLS[name]:COLS[name] + 8], ALU.add, ALU.mult).then_inc(gain_done, 1)
            dve.wait_ge(gain_done, 2)

            def rms_modulate(a_, g, src, dst):
                dve.wait_ge(rms_sqrt, a_ + 1)
                dve.reciprocal(rstd[:, :], rstd[:, :]).then_inc(rms_rec, 1)
                dve.wait_ge(rms_rec, a_ + 1)
                for k in range(KT):
                    dve.scalar_tensor_tensor(dst[:, k, :], src[:, k, :], gs[:, g, k:k + 1], rstd[:, :],
                                             ALU.mult, ALU.mult).then_inc(h_pre, 1)
                    dve.wait_ge(h_pre, KT * g + k + 1)
                    dve.tensor_scalar(dst[:, k, :], dst[:, k, :], mod[:, 24 * g + k:24 * g + k + 1], None, ALU.add)\
                        .then_inc(h_done, 1)

            rms_modulate(2, 0, xT, tiles(2))
            for m in range(16, 24):
                head_scale(m, tiles(1)[:, m - 16, :], col("q_g_2" if m < 20 else "k_g_2"))
            for j in range(8):
                i, t = divmod(j, 4)
                c, u = tmp[:, j % 2, :], tiles(4)[:, j, :]
                dve.wait_ge(evac[t], evacs(block_no(QKM, i) + 1))
                if j >= 2:
                    dve.wait_ge(silu_qk, j - 1)
                dve.tensor_scalar(c, u, col("conv_w_2", 24 + j), None, ALU.mult).then_inc(conv2, 1)
                for back in (1, 2, 3):
                    dve.wait_ge(conv2, 4 * j + back)
                    dve.scalar_tensor_tensor(c[:, back:S], u[:, 0:S - back], col("conv_w_2", 8 * (3 - back) + j),
                                             c[:, back:S], ALU.mult, ALU.add).then_inc(conv2, 1)
            dve.wait_ge(consts2, 7)
            for g, row in enumerate((row_b, row_f)):
                dve.wait_ge(gate_mm, g + 1)
                dve.tensor_scalar(row, PS[0:NML, 4 + g, :], par[0:NML, COLS["b_i"] + g:COLS["b_i"] + g + 1], None, ALU.add)\
                    .then_inc(gate_row, 1)
            dve.wait_ge(gate_act, 3)
            dve.wait_ge(gate_row, 2)
            dve.scalar_tensor_tensor(row_f, row_f, 0.0, row_a, ALU.min, ALU.subtract).then_inc(gate_row, 1)
            dve.wait_ge(gate_row, 3)
            dve.tensor_tensor_scan(row_a, row_one, row_f, 0.0, ALU.mult, ALU.add).then_inc(gate_row, 1)
            dve.wait_ge(gate_row, 4)
            dve.tensor_tensor(row_b, row_b, row_a, ALU.subtract).then_inc(gate_row, 1)
            dve.wait_ge(gate_row, 5)
            dve.tensor_tensor_scan(row_c, row_b, row_b, 0.0, ALU.max, ALU.max).then_inc(gate_row, 1)
            dve.wait_ge(gate_row, 6)
            dve.tensor_scalar(row_negc, row_c, -1.0, None, ALU.mult).then_inc(gate_row, 1)
            dve.tensor_tensor(row_m, row_a, row_c, ALU.add).then_inc(gate_row, 1)
            dve.wait_ge(b_xpose, 1)
            dve.tensor_copy(b_cols[:, :, :], PS[:, 4, 0:TT * NML].rearrange("p (t h) -> p t h", h=NML)).then_inc(gate_row, 1)

            dve.wait_ge(consts2, 12)
            dve.wait_ge(gate_row, 9)
            R0 = 3 * 512

            def logits_in(c):
                dve.wait_ge(z_mm, c + 1)
                if c >= 3:
                    dve.wait_ge(sb_exp, c - 2)
                dve.scalar_tensor_tensor(zbuf[c % 3], PSF[:, 0:NCAUSAL], HD2 ** -0.5, neg_strict, ALU.mult, ALU.add)\
                    .then_inc(z_in, 1)

            def softplus(c):
                dve.wait_ge(sb_ln, 3 * c + 3)
                dve.scalar_tensor_tensor(abuf[c % 3], zbuf[c % 3], 0.0, abuf[c % 3], ALU.max, ALU.add).then_inc(sb_sp, 1)

            logits_in(0)
            logits_in(1)
            softplus(0)
            for c in range(NH2):
                zb = zbuf[c % 3]
                dve.wait_ge(r_mm, c + 1)
                dve.tensor_tensor(zb, zb, PSF[:, R0:R0 + NCAUSAL], ALU.subtract).then_inc(sb_arg, 1)
                if c + 1 < NH2:
                    softplus(c + 1)
                if c + 2 < NH2:
                    logits_in(c + 2)
                if c % 2 and c >= 3:
                    pair = (c - 3) // 2
                    dve.wait_ge(y_mm, 2 * pair + 2)
                    dve.tensor_copy(tiles(7)[:, pair, :], PS[:, 6 + pair % 2, :]).then_inc(y2_copy, 1)
            dve.wait_ge(y_mm, NH2)
            dve.tensor_copy(tiles(7)[:, NH2 // 2 - 1, :], PS[:, 6 + (NH2 // 2 - 1) % 2, :]).then_inc(y2_copy, 1)
            def ml_weights(e):
                zb = zbuf[e % 2]
                dve.wait_ge(ml_bc, e + 1)
                if e >= 2:
                    dve.wait_ge(ml_p, e - 1)
                for kt in range(TT):
                    dve.scalar_tensor_tensor(zb[:, causal(kt)], PS[:, 3, kt * P:S], b_cols[:, kt, e:e + 1],
                                             neg_after[:, causal(kt)], ALU.add, ALU.add).then_inc(ml_arg, 1)

            def ml_product(e):
                dve.wait_ge(ml_exp, e + 1)
                dve.wait_ge(ml_qk, e + 1)
                if e >= 2:
                    dve.wait_ge(ml_mm, e - 1)
                dve.scalar_tensor_tensor(abuf[e % 2], PSF[:, 0:NCAUSAL], HDML ** -0.5, zbuf[e % 2], ALU.mult, ALU.mult)\
                    .then_inc(ml_p, 1)

            dve.wait_ge(consts2, 17)
            ml_weights(0)
            ml_product(0)
            for e in range(NML):
                if e + 1 < NML:
                    ml_weights(e + 1)
                    ml_product(e + 1)
                dve.wait_ge(ml_abs, e + 1)
                dve.tensor_tensor(rt[:, e % 2, :], rt[:, e % 2, :], sq[:, e % 2, :], ALU.max).then_inc(ml_max, 1)
                dve.wait_ge(ml_max, e + 1)
                dve.reciprocal(rt[:, e % 2, :], rt[:, e % 2, :]).then_inc(ml_rec, 1)
                dve.wait_ge(ml_rec, e + 1)
                dve.tensor_tensor(tiles(7)[:, 4 + e, :], PS[:, 6, :], rt[:, e % 2, :], ALU.mult).then_inc(ml_y, 1)
            dve.wait_ge(ml_y, NML)
            for m in range(24, 32):
                head_scale(m, tiles(7)[:, m - 24, :], col("g_out_sb", m - 24))
                if m >= 28:
                    dve.wait_ge(hn_done, m + 1)
                    dve.tensor_tensor(tiles(7)[:, m - 24, :], tiles(7)[:, m - 24, :], tiles(6)[:, m - 28, :], ALU.mult)\
                        .then_inc(mixed_gain, 1)
            for i in range(2):
                for t in range(4):
                    j = 4 * i + t
                    done(WO2, i, t)
                    dve.scalar_tensor_tensor(xT[:, j, :], PS[:, t, :], mod[:, 16 + j:17 + j], xT[:, j, :],
                                             ALU.mult, ALU.add).then_inc(evac[t], 1)
            rms_modulate(3, 1, xT, tiles(2))
            for m in range(16):
                for tt in range(TT):
                    n, at = 16 * tt + m, 5 * (TT * m + tt)
                    sc, v8, i8 = scores_sb[:, n, :], top_v[:, n, :], top_i[:, n, :]
                    dve.wait_ge(sc_done, m + 1)
                    dve.max(v8[:, 0:8], sc).then_inc(top_done, 1)
                    dve.wait_ge(top_done, at + 1)
                    dve.max_index(i8[:, 0:8], v8[:, 0:8], sc).then_inc(top_done, 1)
                    dve.wait_ge(top_done, at + 2)
                    dve.match_replace(sc, v8[:, 0:8], sc, NEG).then_inc(top_done, 1)
                    dve.wait_ge(top_done, at + 3)
                    dve.max(v8[:, 8:16], sc).then_inc(top_done, 1)
                    dve.wait_ge(top_done, at + 4)
                    dve.max_index(i8[:, 8:16], v8[:, 8:16], sc).then_inc(top_done, 1)
            dve.wait_ge(top_done, 5 * 64)
            dve.wait_ge(consts2, 18)
            dve.memset(zero_row[:, :], 0.0).then_inc(fin_a, 1)

            top4 = slots[:, 3, 0:1024]
            topi4 = slots[:, 3, 1024:2048].bitcast(U32)
            square = [P, TOPK, TOPK]

            def held_until(s_, value):
                dve.wait_ge(s_, value)
                dve.sem_inc(held, 1)

            def routing(item, first=False):
                if not first:
                    dve.wait_ge(routed, item)
                side_v = [top4[:, bass.ds(32 * item + 16 * s_, 16)] for s_ in range(2)]
                dve.tensor_tensor(cand.rearrange("p (i j) -> p i j", j=TOPK), side_v[0].unsqueeze(2).broadcast_to(square),
                                  side_v[1].unsqueeze(1).broadcast_to(square), ALU.add).then_inc(cand_done, 1)
                held_until(cand_done, item + 1)
                dve.max(best_v[:, 0:8], cand).then_inc(best_done, 1)
                held_until(best_done, 5 * item + 1)
                dve.max_index(best_p[:, 0:8], best_v[:, 0:8], cand).then_inc(best_done, 1)
                held_until(best_done, 5 * item + 2)
                dve.match_replace(cand, best_v[:, 0:8], cand, NEG).then_inc(best_done, 1)
                held_until(best_done, 5 * item + 3)
                dve.max(best_v[:, 8:16], cand).then_inc(best_done, 1)
                held_until(best_done, 5 * item + 4)
                dve.max_index(best_p[:, 8:16], best_v[:, 8:16], cand).then_inc(best_done, 1)
                dve.tensor_scalar(soft_e, best_v, best_v[:, 0:1], None, ALU.subtract).then_inc(gate_arg, 1)
                dve.wait_ge(best_done, 5 * item + 5)
                dve.tensor_scalar(pos[:, 0, :], best_p, 4, None, ALU.logical_shift_right).then_inc(picked, 1)
                dve.tensor_scalar(pos[:, 1, :], best_p, 15, None, ALU.bitwise_and).then_inc(picked, 1)
                dve.wait_ge(picked, 5 * item + 2)
                oh = onehot.rearrange("p (s k) -> p s k", k=16)
                oh4 = onehot.rearrange("p (s k i) -> p s k i", k=TOPK, i=16)
                dve.tensor_tensor(oh, pos.rearrange("p s k -> p (s k)").unsqueeze(2).broadcast_to([P, 32, 16]),
                                  iota16[:, :].unsqueeze(1).broadcast_to([P, 32, 16]), ALU.is_equal).then_inc(picked, 1)
                dve.wait_ge(picked, 5 * item + 3)
                keys = topi4[:, bass.ds(32 * item, 32)].rearrange("p (s i) -> p s i", s=2)
                dve.tensor_tensor(oh4, oh4, keys.unsqueeze(2).broadcast_to([P, 2, TOPK, 16]), ALU.mult).then_inc(picked, 1)
                dve.wait_ge(picked, 5 * item + 4)
                dve.tensor_reduce(picks.rearrange("p s k -> p (s k)"), oh, AX.X, ALU.add).then_inc(picked, 1)
                dve.wait_ge(gate_exp, item + 1)
                dve.reciprocal(soft_sum[:, 1:2], soft_sum[:, 0:1]).then_inc(gate_inv, 1)
                dve.wait_ge(gate_inv, item + 1)
                dve.tensor_scalar(gates[:, bass.ds(16 * item, 16)], soft_e, soft_sum[:, 1:2], None, ALU.mult).then_inc(gated, 1)
                dve.wait_ge(picked, 5 * item + 5)
                dve.scalar_tensor_tensor(experts[:, bass.ds(16 * item, 16)], picks[:, 0, :], float(NK), picks[:, 1, :],
                                         ALU.mult, ALU.add).then_inc(routed, 1)

            def turn(tt, it, first=False, last=False):
                if not last:
                    routing(it + 1)

                def dot(r):
                    dve.wait_ge(u_in[r % 8], 32 * it + 16 * (r // 8) + 16)
                    if not first or r >= 4:
                        dve.wait_ge(dot_done, 16 * it + r - 3)
                    dve.tensor_tensor_reduce(out=product[r % 4], in0=u_ring[r % 8], in1=h2_tok[:, tt, :], scale=1.0,
                                             scalar=0.0, op0=ALU.mult, op1=ALU.add, accum_out=dots[:, r:r + 1])\
                        .then_inc(dot_done, 1)

                def coefficients(q):
                    dve.wait_ge(gelu_done, 4 * it + q + 1)
                    dve.wait_ge(gated, it + 1)
                    if not first:
                        dve.wait_ge(diag_done, 16 * it + 4 * q - 12)
                    dve.tensor_tensor(coef[:, 4 * q:4 * q + 4], acts[:, 4 * q:4 * q + 4],
                                      gates[:, bass.ds(16 * it + 4 * q, 4)], ALU.mult).then_inc(coef_done, 1)

                for q in range(4):
                    for j in range(4):
                        dot(4 * q + j)
                    if q:
                        coefficients(q - 1)
                coefficients(3)

            dve.wait_ge(tok_copy, 18)
            routing(0, first=True)
            for tt in range(TT):
                expert_turns(dve, tt, turn, last_apart=True)
                dve.wait_ge(moe_mm, NSLOT * (tt + 1))
                y = PS[:, 2 * (tt % 2):2 * (tt % 2) + 2, :].rearrange("p b n -> p (b n)")
                dve.wait_ge(dot_done, NSLOT * (tt + 1))
                dve.tensor_tensor(product[0], y, gate2, ALU.mult).then_inc(fin_a, 1)
                dve.wait_ge(fin_a, tt + 2)
                dve.tensor_tensor(x_tok[:, tt, :], x_tok[:, tt, :], product[0], ALU.add).then_inc(fin_b, 1)
                dve.wait_ge(fin_b, tt + 1)


INPUTS = ["x", "w_in", "rel_bias", "w_attn_proj", "w_conv_proj", "w_gate", "w_out", "w_up", "w_down", "w_ada_2",
          "w_in_2", "w_out_2", "w_q_peer_2", "sub_keys_2", "expert_u_2", "expert_v_2"]


def kernel(**inputs):
    import numpy as np
    import concourse.bacc as bacc
    from concourse.bass_utils import run_bass_kernel_spmd as run

    nc = bacc.Bacc("TRN2", target_bir_lowering=False, num_devices=1)
    arrays = {}
    for name in INPUTS:
        v = np.asarray(inputs[name])
        if name.endswith("_2"):
            v = v[0]
        arrays[name] = np.ascontiguousarray(v)
    def columns(v):
        return np.asarray(v).reshape(-1, 128).T

    def pad4(v):
        return np.concatenate([np.asarray(v).reshape(4, 1), np.zeros((124, 1), np.float32)])

    def twice(v):
        return np.tile(np.asarray(v).reshape(64, 1), (2, 1))

    parts = {"norm1": columns(inputs["norm1_g"]), "conv_w": columns(inputs["conv_w"]),
             "conv_b": columns(inputs["conv_b"]), "b_gate": columns(inputs["b_gate"]),
             "norm2": columns(inputs["norm2_g"]), "c": columns(inputs["c_2"]), "b_ada": columns(inputs["b_ada_2"]),
             "norm1_2": columns(inputs["g_norm1_2"]), "norm2_2": columns(inputs["g_norm2_2"]),
             "conv_w_2": columns(inputs["conv_w_2"]), "g_out_sb": columns(inputs["g_out_sb_2"]),
             "g_out_ml": columns(inputs["g_out_ml_2"]), "q_g": twice(inputs["q_norm_g"]),
             "k_g": twice(inputs["k_norm_g"]), "q_g_2": twice(inputs["g_q_sb_2"]), "k_g_2": twice(inputs["g_k_sb_2"]),
             "b_i": pad4(inputs["b_igate_2"]), "b_f": pad4(inputs["b_fgate_2"])}
    arrays["params"] = np.ascontiguousarray(np.concatenate([parts[name] for name in COLS], axis=1))
    arrays = {f"in_{k}": v for k, v in arrays.items()}
    aps = {k[3:]: nc.dram_tensor(k, v.shape, F32, kind="ExternalInput").ap() for k, v in arrays.items()}
    out = nc.dram_tensor("out", (1, S, D), F32, kind="ExternalOutput").ap()
    build(nc, aps, out)
    r = run(nc, [arrays], core_ids=[0])
    return r.results[0]["out"]
```
